# Optimizing a Trainium2 kernel written in Bass

```python
import math
import jax
import jax.numpy as jnp
from jax import lax
import numpy as np

D_MODEL = 2048
BATCH = 1
SEQ = 1024
DEPTH = 1

D_MIX = D_MODEL
D_ATT = D_MIX // 2
ATT_HEAD_DIM = 128
ATT_HEADS = D_ATT // ATT_HEAD_DIM
ROT_DIM = ATT_HEAD_DIM // 4
ROPE_THETA = 500000.0
DILATED_PATTERNS = ((128, 1), (512, 4), (2048, 16))

D_MLSTM = D_MIX - D_ATT
M_HEADS = 4
M_V_DIM = D_MLSTM // M_HEADS
M_QK_DIM = M_V_DIM // 2
M_CHUNK = 64
N_GATES = 4

SPLITS = (D_ATT, D_ATT, D_ATT, D_ATT,
          M_HEADS * M_QK_DIM, M_HEADS * M_QK_DIM,
          D_MLSTM, D_MLSTM, D_MLSTM,
          N_GATES * M_HEADS)
D_IN = sum(SPLITS)

NORM_EPS = 1e-6
NEG = -1e30

kernel_name = "hybrid_dilated_attn_mlstm_encoder"

def _rmsnorm(x, w):
    xf = x.astype(jnp.float32)
    return xf * lax.rsqrt(jnp.mean(xf * xf, axis=-1, keepdims=True) + NORM_EPS) * w.astype(jnp.float32)

def _rope_partial(x, cos, sin):
    half = ROT_DIM // 2
    x1 = x[..., :half]
    x2 = x[..., half:ROT_DIM]
    c = cos[None, :, None, :]
    s = sin[None, :, None, :]
    rot = jnp.concatenate([x1 * c - x2 * s, x2 * c + x1 * s], axis=-1)
    return jnp.concatenate([rot, x[..., ROT_DIM:]], axis=-1)

def _dilated_band_attention(q, k, v, dil, n_side):
    B, S, H, hd = q.shape
    L = S // dil
    qb = n_side
    nb = -(-L // qb)
    Lp = nb * qb

    def to_res(t):
        return t.reshape(B, L, dil, H, hd).transpose(0, 2, 3, 1, 4)

    qr = jnp.pad(to_res(q), ((0, 0), (0, 0), (0, 0), (0, Lp - L), (0, 0)))
    qr = qr.reshape(B, dil, H, nb, qb, hd)

    def bands(t):
        tp = jnp.pad(t, ((0, 0), (0, 0), (0, 0), (qb, Lp - L + qb), (0, 0)))
        tp = tp.reshape(B, dil, H, nb + 2, qb, hd)
        return jnp.concatenate([tp[:, :, :, :-2], tp[:, :, :, 1:-1], tp[:, :, :, 2:]], axis=4)

    kb = bands(to_res(k))
    vb = bands(to_res(v))
    q_idx = jnp.arange(nb)[:, None] * qb + jnp.arange(qb)[None, :]
    k_idx = jnp.arange(nb)[:, None] * qb - qb + jnp.arange(3 * qb)[None, :]
    rel = k_idx[:, None, :] - q_idx[:, :, None]
    valid = (jnp.abs(rel) <= n_side) & (k_idx[:, None, :] >= 0) & (k_idx[:, None, :] < L)

    scores = jnp.einsum('brhnqc,brhnkc->brhnqk', qr, kb) * (hd ** -0.5)
    scores = jnp.where(valid, scores, NEG)
    m = jnp.max(scores, axis=-1, keepdims=True)
    p = jnp.exp(scores - m)
    l = jnp.sum(p, axis=-1, keepdims=True)
    o = jnp.einsum('brhnqk,brhnkc->brhnqc', p, vb) / l
    lse = (m + jnp.log(l))[..., 0]

    o = o.reshape(B, dil, H, Lp, hd)[:, :, :, :L].transpose(0, 3, 1, 2, 4).reshape(B, S, H, hd)
    lse = lse.reshape(B, dil, H, Lp)[..., :L].transpose(0, 3, 1, 2).reshape(B, S, H)
    return o, lse

def _mlstm_chunkwise(q, k, v, log_i, log_f):
    B, H, S, dk = q.shape
    dv = v.shape[-1]
    nc = S // M_CHUNK

    def chunks(t):
        return jnp.moveaxis(t.reshape(B, H, nc, M_CHUNK, *t.shape[3:]), 2, 0)

    xs = (chunks(q), chunks(k), chunks(v), chunks(log_i), chunks(log_f))
    tril = jnp.tril(jnp.ones((M_CHUNK, M_CHUNK), dtype=bool))

    def step(carry, inp):
        C, n, m = carry
        qc, kc, vc, lic, lfc = inp
        b = jnp.cumsum(lfc, axis=-1)
        D = b[..., :, None] - b[..., None, :] + lic[..., None, :]
        D = jnp.where(tril, D, NEG)
        inter = b + m[..., None]
        m_row = jnp.maximum(inter, jnp.max(D, axis=-1))
        w_intra = jnp.exp(D - m_row[..., None])
        w_inter = jnp.exp(inter - m_row)
        s = jnp.einsum('bhtd,bhsd->bhts', qc, kc) * w_intra
        num = w_inter[..., None] * jnp.einsum('bhtd,bhde->bhte', qc, C) \
            + jnp.einsum('bhts,bhse->bhte', s, vc)
        den = w_inter * jnp.einsum('bhtd,bhd->bht', qc, n) + jnp.sum(s, axis=-1)
        h = num / jnp.maximum(jnp.abs(den), jnp.exp(-m_row))[..., None]
        bL = b[..., -1]
        g = bL[..., None] - b + lic
        m_new = jnp.maximum(bL + m, jnp.max(g, axis=-1))
        decay = jnp.exp(bL + m - m_new)
        wk = jnp.exp(g - m_new[..., None])
        C_new = decay[..., None, None] * C + jnp.einsum('bhs,bhsd,bhse->bhde', wk, kc, vc)
        n_new = decay[..., None] * n + jnp.einsum('bhs,bhsd->bhd', wk, kc)
        return (C_new, n_new, m_new), h

    init = (jnp.zeros((B, H, dk, dv), jnp.float32),
            jnp.zeros((B, H, dk), jnp.float32),
            jnp.full((B, H), NEG, jnp.float32))
    _, hs = lax.scan(step, init, xs)
    return jnp.moveaxis(hs, 0, 2).reshape(B, H, S, dv)

def _hybrid_layer(x, norm_w, w_in, b_gates, q_norm_w, k_norm_w, m_norm_w, w_out, cos, sin):
    B, S, _ = x.shape
    h = _rmsnorm(x, norm_w).astype(x.dtype)
    proj = jnp.einsum('bsd,df->bsf', h, w_in)
    offsets = np.cumsum(SPLITS)[:-1].tolist()
    q_a, k_a, v_a, z_a, q_m, k_m, v_m, o_m, z_m, g = jnp.split(proj, offsets, axis=-1)

    qa = _rope_partial(_rmsnorm(q_a.reshape(B, S, ATT_HEADS, ATT_HEAD_DIM), q_norm_w), cos, sin)
    ka = _rope_partial(_rmsnorm(k_a.reshape(B, S, ATT_HEADS, ATT_HEAD_DIM), k_norm_w), cos, sin)
    va = v_a.reshape(B, S, ATT_HEADS, ATT_HEAD_DIM).astype(jnp.float32)
    outs, lses = [], []
    for window, dil in DILATED_PATTERNS:
        o, lse = _dilated_band_attention(qa, ka, va, dil, window // (2 * dil))
        outs.append(o)
        lses.append(lse)
    mix_w = jax.nn.softmax(jnp.stack(lses, axis=0), axis=0)
    attn = jnp.sum(mix_w[..., None] * jnp.stack(outs, axis=0), axis=0).reshape(B, S, D_ATT)
    attn = attn * jax.nn.silu(z_a.astype(jnp.float32))

    qm = q_m.reshape(B, S, M_HEADS, M_QK_DIM).astype(jnp.float32).transpose(0, 2, 1, 3)
    km = (k_m.reshape(B, S, M_HEADS, M_QK_DIM).astype(jnp.float32) * (M_QK_DIM ** -0.5)).transpose(0, 2, 1, 3)
    vm = v_m.reshape(B, S, M_HEADS, M_V_DIM).astype(jnp.float32).transpose(0, 2, 1, 3)
    gates = (g.astype(jnp.float32) + b_gates.astype(jnp.float32)).reshape(B, S, N_GATES, M_HEADS)
    gates = gates.transpose(2, 0, 3, 1)
    i_fwd, f_fwd, i_bwd, f_bwd = gates[0], gates[1], gates[2], gates[3]
    h_fwd = _mlstm_chunkwise(qm, km, vm, i_fwd, jax.nn.log_sigmoid(f_fwd))
    flip = lambda t: jnp.flip(t, axis=2)
    h_bwd = flip(_mlstm_chunkwise(flip(qm), flip(km), flip(vm), flip(i_bwd),
                                  flip(jax.nn.log_sigmoid(f_bwd))))
    hm = (h_fwd + h_bwd).transpose(0, 2, 1, 3)
    hm = _rmsnorm(hm, m_norm_w.reshape(M_HEADS, M_V_DIM)).reshape(B, S, D_MLSTM)
    hm = jax.nn.sigmoid(o_m.astype(jnp.float32)) * hm * jax.nn.silu(z_m.astype(jnp.float32))

    y = jnp.concatenate([attn, hm], axis=-1).astype(x.dtype)
    return jnp.einsum('bsf,fd->bsd', y, w_out)

def setup_inputs(seed: int = 0) -> dict:
    key = jax.random.key(seed)
    ks = jax.random.split(key, 12)
    f32 = jnp.float32
    x = jax.random.normal(ks[0], (BATCH, SEQ, D_MODEL), f32)
    norm_w = 1.0 + 0.02 * jax.random.normal(ks[1], (DEPTH, D_MODEL), f32)
    w_in = jax.random.normal(ks[2], (DEPTH, D_MODEL, D_IN), f32) * (D_MODEL ** -0.5)
    i_bias = 0.1 * jax.random.normal(ks[3], (DEPTH, 2, M_HEADS), f32)
    f_bias = jnp.linspace(3.0, 6.0, M_HEADS, dtype=f32)[None, None, :] \
        + 0.1 * jax.random.normal(ks[4], (DEPTH, 2, M_HEADS), f32)
    b_gates = jnp.stack([i_bias[:, 0], f_bias[:, 0], i_bias[:, 1], f_bias[:, 1]], axis=1)
    b_gates = b_gates.reshape(DEPTH, N_GATES * M_HEADS)
    q_norm_w = 1.0 + 0.02 * jax.random.normal(ks[5], (DEPTH, ATT_HEAD_DIM), f32)
    k_norm_w = 1.0 + 0.02 * jax.random.normal(ks[6], (DEPTH, ATT_HEAD_DIM), f32)
    m_norm_w = 1.0 + 0.02 * jax.random.normal(ks[7], (DEPTH, D_MLSTM), f32)
    w_out = jax.random.normal(ks[8], (DEPTH, D_MIX, D_MODEL), f32) * (D_MIX ** -0.5)
    return {"x": x, "norm_w": norm_w, "w_in": w_in, "b_gates": b_gates,
            "q_norm_w": q_norm_w, "k_norm_w": k_norm_w, "m_norm_w": m_norm_w,
            "w_out": w_out}

def reference(x, norm_w, w_in, b_gates, q_norm_w, k_norm_w, m_norm_w, w_out):
    S = x.shape[1]
    pos = jnp.arange(S, dtype=jnp.float32)
    inv_freq = ROPE_THETA ** (-jnp.arange(0, ROT_DIM, 2, dtype=jnp.float32) / ROT_DIM)
    ang = pos[:, None] * inv_freq[None, :]
    cos, sin = jnp.cos(ang), jnp.sin(ang)
    for layer in range(DEPTH):
        x = x + _hybrid_layer(x, norm_w[layer], w_in[layer], b_gates[layer],
                              q_norm_w[layer], k_norm_w[layer], m_norm_w[layer],
                              w_out[layer], cos, sin)
    return x


_drawn_inputs = setup_inputs


def setup_inputs(seed=0):
    import zlib

    import numpy as np

    out = dict(_drawn_inputs(seed))
    spreads = {}
    factors = {'norm_w': 3.893, 'q_norm_w': 8.0, 'k_norm_w': 8.0, 'm_norm_w': 8.0}
    for name, (base, spread) in spreads.items():
        noise = np.random.default_rng([zlib.crc32(name.encode()), seed]).standard_normal(out[name].shape)
        drawn = base * np.exp(spread * noise) if base else spread * noise
        out[name] = jnp.asarray(drawn.astype(out[name].dtype))
    for name, factor in factors.items():
        out[name] = (out[name] * factor).astype(out[name].dtype)
    return out
```

```python
from contextlib import ExitStack

import numpy as np

import concourse.bass as bass
from concourse import mybir

F32 = mybir.dt.float32
F32R = mybir.dt.float32r
ALU = mybir.AluOpType
ACT = mybir.ActivationFunctionType

P = 128
D_MODEL = 2048
SEQ = 1024
KT = D_MODEL // P
HALF = 512
TB = SEQ // P
PIECES = 4
KP = KT // PIECES
LEAD = 2

ATT_HEADS = 8
ROT = 32
M_HEADS = 4
A_TILES = 4
M_TILES = 8
A_PIECES = A_TILES * PIECES
M_PIECES = M_TILES * PIECES
G_PIECE = PIECES
A_PIECE = G_PIECE + M_HEADS * M_PIECES
O_PIECE = A_PIECE + ATT_HEADS * A_PIECES
O_TILES = D_MODEL // P
N_PIECE = O_PIECE + O_TILES * PIECES
G_TILE, A_TILE, O_TILE = G_PIECE // PIECES, A_PIECE // PIECES, O_PIECE // PIECES

EPS = 1e-6
NEG = -1e30
V1 = 258
MV = 257
STEPS = 2 * TB
MASK_W = SEQ + P * (TB - 1)


def chunk_of(n):
    return n if n < TB else STEPS - 1 - n


def build_program(nc, xT, w_all, vecs, norm_cols, m_cols, att_mask, rope, eye, tri, y_dram, outT):
    with ExitStack() as ctx:
        def sb(name, shape, dt=F32):
            return ctx.enter_context(nc.sbuf_tensor(name, shape, dt))

        def sem(name):
            return ctx.enter_context(nc.semaphore(name))

        h_hi = sb("h_hi", [P, KT, SEQ], F32R)
        h_lo = sb("h_lo", [P, KT, SEQ], F32R)
        w_raw = sb("w_raw", [P, PIECES, KP * P])
        w_hi = sb("w_hi", [P, PIECES, KP * P], F32R)
        w_lo = sb("w_lo", [P, PIECES, KP * P], F32R)
        ident = sb("ident", [P, P])
        ones = sb("ones", [P, P])
        vec = sb("vec", [P, 8])
        ncol = sb("ncol", [P, KT])
        mcol = sb("mcol", [P, 8])
        tri_m = sb("tri_m", [P, 2, P])
        small = sb("small", [P, 64])
        g_cols = sb("g_cols", [P, TB, 2, M_HEADS])
        e_cols = sb("e_cols", [P, TB, 2, M_HEADS])
        A_FL = 12672
        arena = sb("arena", [P, A_FL])

        def view(at, n):
            return arena[:, at:at + n]

        qT, kT = view(0, 1024), view(1024, 1024)
        hbuf = view(2048, 2048)
        gate = view(4096, 2048)
        vst = view(6144, 1024)
        v1 = view(7168, TB * V1).rearrange("p (c e) -> p c e", e=V1)
        rows = view(9232, 1024)
        chunkbuf = view(10256, 2 * 4 * P).rearrange("p (i k t) -> p i k t", i=2, k=4)
        cst = view(11280, 2 * V1).rearrange("p (i e) -> p i e", e=V1)
        sel = view(11796, 4 * P).rearrange("p (d t) -> p d t", d=4)
        gc = view(12308, 2 * TB).rearrange("p (c d) -> p c d", d=2)
        ec = view(12324, 2 * TB).rearrange("p (c d) -> p c d", d=2)
        zg = view(2048, 1024)
        zst = view(3072, 1024)
        prob = view(4096, 2048).rearrange("p (i k) -> p i k", i=2)
        vtok = view(7168, 1024).rearrange("p (b d) -> p b d", d=P)
        pT = view(8192, 2048).rearrange("p (b q) -> p b q", b=TB)
        cos, sin = view(8192, 1024), view(9216, 1024)
        amask = view(10240, MASK_W)
        gr = [view(2048 + 1024 * i, 1024) for i in range(4)] + [qT, kT]
        xblk = view(0, 4 * SEQ).rearrange("p (i t) -> p i t", i=4)
        hblk = view(4096, 4 * SEQ).rearrange("p (i t) -> p i t", i=4)
        xrs = view(8192, 1024)
        oblk = view(0, 2 * SEQ).rearrange("p (i t) -> p i t", i=2)
        xres = view(2048, 2 * SEQ).rearrange("p (i t) -> p i t", i=2)
        yblk = view(7168, 2 * SEQ).rearrange("p (i t) -> p i t", i=2)

        ps = ctx.enter_context(nc.psum_tensor("ps", [P, 8, HALF], F32))
        psP = ps[:, 0:2, :]
        psS = ps[:, 4:6, :].rearrange("p b k -> p (b k)")

        def flat(b):
            return ps[:, b:b + 2, :].rearrange("p b k -> p (b k)")

        w_landed = [sem(f"w_landed{i}") for i in range(PIECES)]
        w_hi_done = sem("w_hi_done")
        w_lo_done = sem("w_lo_done")
        w_used = sem("w_used")
        proj_done = sem("proj_done")
        proj_free = sem("proj_free")
        consts = sem("consts")
        ones_set = sem("ones_set")
        x_in = [sem(f"x_in{i}") for i in range(4)]
        x_sq = sem("x_sq")
        x_sum = sem("x_sum")
        x_rms = sem("x_rms")
        x_rs = sem("x_rs")
        h_full = sem("h_full")
        h_hid = sem("h_hid")
        h_lod = sem("h_lod")
        prep = sem("prep")
        g_act = sem("g_act")
        g_dve = sem("g_dve")
        g_pe = sem("g_pe")
        m_sel = sem("m_sel")
        m_pick = sem("m_pick")
        m_vst = sem("m_vst")
        m_vtr = sem("m_vtr")
        m_va = sem("m_va")
        m_vd = sem("m_vd")
        m_qk = sem("m_qk")
        m_x = sem("m_x")
        m_t = sem("m_t")
        m_w = sem("m_w")
        m_ops = sem("m_ops")
        m_kw = sem("m_kw")
        m_num = sem("m_num")
        m_upd = sem("m_upd")
        m_c = sem("m_c")
        m_den = sem("m_den")
        m_h = sem("m_h")
        m_gate = sem("m_gate")
        m_g = sem("m_g")
        m_ss = sem("m_ss")
        m_rms = sem("m_rms")
        m_rs = sem("m_rs")
        m_hn = sem("m_hn")
        m_htr = sem("m_htr")
        m_y = sem("m_y")
        m_out = sem("m_out")
        p_held = sem("p_held")
        a_qk_out = sem("a_qk_out")
        a_sq = sem("a_sq")
        a_ssum = sem("a_ssum")
        a_rms = sem("a_rms")
        a_rope = sem("a_rope")
        a_cs = sem("a_cs")
        a_s = sem("a_s")
        a_m = sem("a_m")
        a_e = sem("a_e")
        a_r = sem("a_r")
        a_p = sem("a_p")
        a_t = sem("a_t")
        a_ta = sem("a_ta")
        a_td = sem("a_td")
        a_pv = sem("a_pv")
        a_y = sem("a_y")
        a_vst = sem("a_vst")
        a_vtr = sem("a_vtr")
        a_va = sem("a_va")
        a_vd = sem("a_vd")
        a_z = sem("a_z")
        a_zg = sem("a_zg")
        a_out = sem("a_out")
        o_in = [sem(f"o_in{i}") for i in range(2)]
        o_hi = sem("o_hi")
        o_lo = sem("o_lo")
        o_x = [sem(f"o_x{i}") for i in range(2)]
        o_done = sem("o_done")
        o_out = [sem(f"o_out{i}") for i in range(2)]

        block = ctx.enter_context(nc.Block())

        @block.sync
        def _(sp):
            sp.dma_start(vec[:], vecs).then_inc(consts, 16)
            sp.dma_start(ncol[:], norm_cols).then_inc(consts, 16)
            sp.dma_start(mcol[:], m_cols).then_inc(consts, 16)
            sp.dma_start(ident[:], eye).then_inc(consts, 16)
            sp.dma_start(tri_m[:], tri).then_inc(consts, 16)
            for rnd in range(2):
                for kt in range(KT):
                    n = rnd * KT + kt
                    if n >= 4 and n - 4 < KT:
                        sp.wait_ge(x_sq, n - 3)
                    if n - 4 >= KT:
                        sp.wait_ge(h_full, n - 4 - KT + 1)
                    sp.dma_start(xblk[:, n % 4, :], xT[kt]).then_inc(x_in[n % 4], 16)
                    if rnd == 0 and kt < PIECES:
                        sp.dma_start(w_raw[:, kt, :], w_all[kt]).then_inc(w_landed[kt], 16)
            with sp.Fori(1, N_PIECE // PIECES) as tile:
                for s in range(PIECES):
                    sp.wait_ge(w_lo_done, (tile - 1) * PIECES + s + 1)
                    sp.dma_start(w_raw[:, s, :], w_all[bass.ds(tile * PIECES + s, 1)].rearrange("a p n -> p (a n)")
                                 ).then_inc(w_landed[s], 16)

        def weight_hi(act, tile, s):
            act.wait_ge(w_landed[s], (tile + 1) * 16)
            if not (isinstance(tile, int) and tile == 0):
                act.wait_ge(w_used, (tile - 1) * PIECES + s + 1)
            nc.scalar.copy(w_hi[:, s, :], w_raw[:, s, :]).then_inc(w_hi_done, 1)

        def weight_lo(dve, tile, s):
            dve.wait_ge(w_hi_done, tile * PIECES + s + 1)
            nc.vector.tensor_tensor(w_lo[:, s, :], w_raw[:, s, :], w_hi[:, s, :].bitcast(F32), ALU.subtract
                                    ).then_inc(w_lo_done, 1)

        def piece(pe, tile, s, per_block=None):
            pe.wait_ge(w_lo_done, tile * PIECES + s + 1)
            if s == 0 and not (isinstance(tile, int) and tile == 0):
                pe.wait_ge(proj_free, tile)
            for j in range(KP):
                kt = s * KP + j
                if per_block is not None:
                    per_block(kt)
                hi = w_hi[:, s, j * P:(j + 1) * P]
                lo = w_lo[:, s, j * P:(j + 1) * P]
                first, last = kt == 0, kt == KT - 1
                for i in range(2):
                    cols = slice(i * HALF, (i + 1) * HALF)
                    nc.tensor.matmul(psP[:, i, :], hi, h_hi[:, kt, cols], start=first, stop=False)
                    nc.tensor.matmul(psP[:, i, :], hi, h_lo[:, kt, cols], start=False, stop=False)
                for i in range(2):
                    cols = slice(i * HALF, (i + 1) * HALF)
                    mm = nc.tensor.matmul(psP[:, i, :], lo, h_hi[:, kt, cols], start=False, stop=last)
            mm.then_inc(w_used, 1)

        def projected(pe):
            pass

        @block.tensor
        def _(pe):
            pe.wait_ge(ones_set, 1)
            pe.wait_ge(consts, 80)
            for kt in range(KT):
                pe.wait_ge(x_sq, kt + 1)
                for i in range(2):
                    mm = nc.tensor.matmul(ps[:, 6 + i, :], ones[:], hblk[:, kt % 4, i * HALF:(i + 1) * HALF],
                                          start=kt == 0, stop=kt == KT - 1)
                mm.then_inc(x_sum, 1)

            def transposes(src, bank, n, done):
                for b in range(n):
                    t = nc.tensor.transpose(ps[:, bank + b // 4, (b % 4) * P:(b % 4 + 1) * P], src(b), ident[:])
                    if b % 4 == 3:
                        t.then_inc(done, 1)

            def block_made(kt):
                pe.wait_ge(h_lod, kt + 1)
            for s in range(PIECES):
                piece(pe, 0, s, block_made)

            def gate_columns():
                pe.wait_ge(g_dve, GD_ROWS)
                for b in range(2 * TB):
                    src = (gr[3] if b < TB else gr[1])[0:64, (b % TB) * P:(b % TB + 1) * P]
                    t = nc.tensor.transpose(ps[:, 4 + b // TB, (b % TB) * 64:(b % TB + 1) * 64], src, ident[0:64, 0:64])
                t.then_inc(g_pe, 1)

            def step_inputs(j, n):
                c, d = chunk_of(n), n // TB
                cols = slice(c * P, (c + 1) * P)
                if n == 0:
                    pe.wait_ge(m_sel, j + 1)
                    pe.wait_ge(m_qk, 2 * j + 2)
                if n > 0 or not isinstance(j, int) or j > 0:
                    pe.wait_ge(m_ops, 16 * j + n)
                    pe.wait_ge(m_kw, 16 * j + n)
                nc.tensor.matmul(ps[:, 6, 0:P], sel[:, 2 * d, :], rows[:, cols], start=True, stop=True)
                nc.tensor.matmul(ps[:, 6, P:2 * P], sel[:, 2 * d + 1, :], rows[:, cols], start=True, stop=True)
                nc.tensor.matmul(ps[:, 6, 2 * P:3 * P], kT[:, cols], qT[:, cols], start=True, stop=True)
                nc.tensor.transpose(ps[:, 7, 0:P], kT[:, cols], ident[:]).then_inc(m_x, 1)

            def step_products(j, n):
                c, i = chunk_of(n), n % 2
                first = n % TB == 0
                pe.wait_ge(m_ops, 16 * j + n + 1)
                if n == 0:
                    pe.wait_ge(m_va, 2 * j + 2)
                    pe.wait_ge(m_vd, 2 * j + 2)
                if n > 0 or not isinstance(j, int) or j > 0:
                    pe.wait_ge(m_h, 16 * j + n)
                mm = nc.tensor.matmul(ps[:, 4, 0:MV], chunkbuf[:, i, 1, :], v1[:, c, 0:MV], start=True, stop=first)
                if not first:
                    pe.wait_ge(m_c, 16 * j + n)
                    mm = nc.tensor.matmul(ps[:, 4, 0:MV], chunkbuf[:, i, 2, :], cst[:, n % 2, 0:MV],
                                          start=False, stop=True)
                mm.then_inc(m_num, 1)
                pe.wait_ge(m_kw, 16 * j + n + 1)
                if first and (n > 0 or not isinstance(j, int) or j > 0):
                    pe.wait_ge(m_c, 16 * j + n)
                nc.tensor.matmul(ps[:, 5, 0:MV], chunkbuf[:, i, 3, :], v1[:, c, 0:MV], start=True, stop=True
                                 ).then_inc(m_upd, 1)

            def m_value_transposes(j, half):
                pe.wait_ge(m_vst, 2 * j + half + 1)
                if half == 1:
                    pe.wait_ge(m_va, 2 * j + 1)
                    pe.wait_ge(m_vd, 2 * j + 1)
                elif not (isinstance(j, int) and j == 0):
                    pe.wait_ge(m_y, 4 * j)
                transposes(lambda b: vst[:, b * P:(b + 1) * P], 2, TB, m_vtr)

            def m_output_transposes(j, e):
                pe.wait_ge(m_hn, 8 * j + 8)
                if e == 1:
                    pe.wait_ge(m_y, 4 * j + 2)
                transposes(lambda b: hbuf[:, b * 256 + e * P:b * 256 + (e + 1) * P], 2, TB, m_htr)

            def mlstm_pe(j, first):
                for u in range(M_PIECES):
                    piece(pe, j * M_TILES + G_TILE + u // PIECES, u % PIECES)
                    if first and u == 4:
                        gate_columns()
                    if not first and u in (1, 2):
                        m_output_transposes(j - 1, u - 1)
                    if u in (4, 8):
                        m_value_transposes(j, u // 4 - 1)
                    if u >= 16:
                        step_products(j, u - 16)
                    if 15 <= u < 31:
                        step_inputs(j, u - 15)

            mlstm_pe(0, True)
            with pe.Fori(1, M_HEADS) as j:
                mlstm_pe(j, False)

            def square_sums(n):
                pe.wait_ge(a_sq, n + 1)
                if not isinstance(n, int) or n > 0:
                    pe.wait_ge(a_rms, n)
                for i in range(2):
                    mm = nc.tensor.matmul(ps[:, 6 + i, :], ones[:], prob[:, 0, i * HALF:(i + 1) * HALF],
                                          start=True, stop=True)
                mm.then_inc(a_ssum, 1)

            def scores(g, i):
                if i == 0:
                    pe.wait_ge(a_rope, 14 * g + 14)
                else:
                    pe.wait_ge(a_m, 8 * g + i)
                for c in range(2):
                    mm = nc.tensor.matmul(ps[:, 4 + c, :], qT[:, i * P:(i + 1) * P], kT[:, c * HALF:(c + 1) * HALF],
                                          start=True, stop=True)
                mm.then_inc(a_s, 1)

            def prob_transposes(g, i):
                pe.wait_ge(a_p, 8 * g + i + 1)
                if i == 0:
                    pe.wait_ge(a_va, g + 1)
                    pe.wait_ge(a_vd, g + 1)
                else:
                    pe.wait_ge(a_ta, 8 * g + i)
                    pe.wait_ge(a_td, 8 * g + i)
                transposes(lambda b: prob[:, i % 2, b * P:(b + 1) * P], 2, TB, a_t)

            def values(g, j, tail):
                if j == 3 and not tail:
                    pe.wait_ge(a_rms, 2 * g + 3)
                pe.wait_ge(a_ta, 8 * g + 2 * j + 2)
                pe.wait_ge(a_td, 8 * g + 2 * j + 2)
                if j > 0:
                    pe.wait_ge(a_y, 4 * g + j)
                for b in range(TB):
                    mm = nc.tensor.matmul(ps[:, 6 + j % 2, 0:256], vtok[:, b, :], pT[:, b, :],
                                          start=b == 0, stop=b == TB - 1)
                mm.then_inc(a_pv, 1)

            def value_transposes(h):
                pe.wait_ge(a_vst, h + 1)
                transposes(lambda b: vst[:, b * P:(b + 1) * P], 2, TB, a_vtr)

            def attention_units(g, u, tail=False):
                if u == 0:
                    square_sums(2 * g + 1)
                if 4 <= u <= 11:
                    scores(g, u - 4)
                if u in (8, 10, 12, 14):
                    values(g, (u - 8) // 2, tail)
                if 6 <= u <= 13:
                    prob_transposes(g, u - 6)

            def attention_pe(h, first):
                for u in range(A_PIECES):
                    piece(pe, h * A_TILES + A_TILE + u // PIECES, u % PIECES)
                    if first and u in (1, 2):
                        m_output_transposes(M_HEADS - 1, u - 1)
                    if not first:
                        attention_units(h - 1, u)
                    if u == 13:
                        if not first:
                            pe.wait_ge(a_y, 4 * h - 1)
                        square_sums(2 * h)
                    if u == 15:
                        value_transposes(h)

            attention_pe(0, True)
            with pe.Fori(1, ATT_HEADS) as h:
                attention_pe(h, False)
            for u in range(A_PIECES):
                attention_units(ATT_HEADS - 1, u, True)

            def y_made(kt):
                pe.wait_ge(o_lo, kt + 1)
            for s in range(PIECES):
                piece(pe, O_TILE, s, y_made)
            with pe.Fori(O_TILE + 1, O_TILE + O_TILES) as tile:
                for s in range(PIECES):
                    piece(pe, tile, s)

        GA_BIAS = 1
        @block.scalar
        def _(act):
            act.wait_ge(prep, 2)
            for kt in range(KT):
                act.wait_ge(x_in[kt % 4], 16 * (kt // 4 + 1))
                if kt >= 4:
                    act.wait_ge(x_sum, kt - 3)
                nc.scalar.activation(hblk[:, kt % 4, :], xblk[:, kt % 4, :], ACT.Square).then_inc(x_sq, 1)
            for s in range(LEAD):
                weight_hi(act, 0, s)
            act.wait_ge(x_sum, KT)
            nc.scalar.activation(xrs[:], flat(6), ACT.Sqrt, bias=vec[:, 4:5], scale=1.0 / D_MODEL).then_inc(x_rms, 1)
            for kt in range(KT):
                act.wait_ge(h_full, kt + 1)
                nc.scalar.copy(h_hi[:, kt, :], hblk[:, kt % 4, :]).then_inc(h_hid, 1)

            def ahead(piece_at):
                tile, s = piece_at
                weight_hi(act, tile + (s + LEAD) // PIECES, (s + LEAD) % PIECES)

            def read_out(tile, out, func=ACT.Copy, scale=1.0, done=None):
                nc.scalar.activation(out, flat(0), func, scale=scale).then_inc(proj_free, 1)

            def tile_end(tile):
                act.wait_ge(w_used, (tile + 1) * PIECES)

            for s in range(PIECES):
                ahead((0, s))
            tile_end(0)
            nc.scalar.activation(gr[0], flat(0), ACT.Identity, bias=vec[:, 2:3]).then_inc(proj_free, 1)

            def gate_rows():
                act.wait_ge(g_dve, GD_SPLIT)
                nc.scalar.activation(gr[4][0:64, :], gr[2][0:64, :], ACT.Abs).then_inc(g_act, 1)
                act.wait_ge(g_act, 1)
                nc.scalar.activation(gr[4][0:64, :], gr[4][0:64, :], ACT.Exp, scale=-1.0).then_inc(g_act, 1)
                act.wait_ge(g_act, 2)
                nc.scalar.activation(gr[4][0:64, :], gr[4][0:64, :], ACT.Ln, bias=1.0).then_inc(g_act, 1)
                act.wait_ge(g_dve, GD_INTER)
                nc.scalar.activation(gr[5][0:64, :], gr[5][0:64, :], ACT.Exp).then_inc(g_act, 1)

            def gate_cols():
                act.wait_ge(g_pe, 1)
                for d in range(2):
                    src = ps[:, 5, :].rearrange("p (c r) -> p c r", r=64)[:, :, 32 * d:32 * d + M_HEADS]
                    nc.scalar.activation(e_cols[:, :, d, :], src, ACT.Exp, scale=-1.0).then_inc(g_act, 1)

            def m_step(j, n):
                c, d, i = chunk_of(n), n // TB, n % 2
                act.wait_ge(m_t, 16 * j + n + 1)
                if n >= 2 or not isinstance(j, int) or j > 0:
                    act.wait_ge(m_upd, 16 * j + n - 1)
                nc.scalar.activation(chunkbuf[:, i, 0, :], chunkbuf[:, i, 0, :], ACT.Exp, bias=gc[:, c, d:d + 1]
                                     ).then_inc(m_w, 1)
                act.wait_ge(m_w, 16 * j + n + 1)
                end = 0 if d else P - 1
                nc.scalar.activation(chunkbuf[:, i, 3, :], ps[:, 7, 0:P], ACT.Copy,
                                     scale=chunkbuf[:, i, 0, end:end + 1]).then_inc(m_kw, 1)

            def mlstm_act(j, first):
                tile0 = j * M_TILES + G_TILE
                for u in range(M_PIECES):
                    ahead((tile0 + u // PIECES, u % PIECES))
                    if first and u == 0:
                        gate_rows()
                    if first and u == 4:
                        gate_cols()
                    if not first and u == 0:
                        m_square_sums(j - 1)
                    if u == 3:
                        tile_end(tile0)
                        if not first:
                            act.wait_ge(m_g, 2 * j)
                        nc.scalar.copy(vst[:], flat(0)).then_inc(m_vst, 1)
                        act.wait_ge(m_vst, 2 * j + 1)
                        act.sem_inc(proj_free, 1)
                    if u in (4, 8):
                        half = u // 4 - 1
                        act.wait_ge(m_vtr, 4 * j + 2 * half + 1)
                        nc.scalar.copy(v1[:, 0:4, half * P:(half + 1) * P], ps[:, 2, :].rearrange("p (b d) -> p b d", d=P)
                                       ).then_inc(m_va, 1)
                    if u == 7:
                        tile_end(tile0 + 1)
                        act.wait_ge(m_vtr, 4 * j + 2)
                        nc.scalar.copy(vst[:], flat(0)).then_inc(m_vst, 1)
                        act.wait_ge(m_vst, 2 * j + 2)
                        act.sem_inc(proj_free, 1)
                    if u == 11:
                        tile_end(tile0 + 2)
                        if first:
                            act.wait_ge(g_dve, GD_ROWS)
                            act.wait_ge(g_pe, 1)
                        nc.scalar.mul(kT[:], flat(0), float(P) ** -0.5).then_inc(m_qk, 1)
                        act.wait_ge(m_qk, 2 * j + 1)
                        act.sem_inc(proj_free, 1)
                    if u == 15:
                        tile_end(tile0 + 3)
                        nc.scalar.copy(qT[:], flat(0)).then_inc(m_qk, 1)
                        act.wait_ge(m_qk, 2 * j + 2)
                        act.sem_inc(proj_free, 1)
                    if u in (19, 23):
                        e = u // 4 - 4
                        tile_end(tile0 + 4 + e)
                        if not first:
                            act.wait_ge(m_out, 16 * j)
                        nc.scalar.activation(gate[:, e * SEQ:(e + 1) * SEQ], flat(0), ACT.Sigmoid).then_inc(m_gate, 1)
                        act.wait_ge(m_gate, 4 * j + e + 1)
                        act.sem_inc(proj_free, 1)
                    if u in (27, 31):
                        e = u // 4 - 6
                        tile_end(tile0 + 6 + e)
                        if e == 0:
                            act.wait_ge(m_vtr, 4 * j + 4)
                        else:
                            act.wait_ge(m_g, 2 * j + 1)
                        nc.scalar.activation(vst[:], flat(0), ACT.Silu).then_inc(m_gate, 1)
                        act.wait_ge(m_gate, 4 * j + 3 + e)
                        act.sem_inc(proj_free, 1)
                    if 15 <= u < 31:
                        m_step(j, u - 15)

            def m_square_sums(j):
                for c in range(TB):
                    if c == 0:
                        act.wait_ge(m_h, 16 * j + 16)
                    nc.scalar.activation(chunkbuf[:, 0, 0:2, :].rearrange("p k t -> p (k t)"),
                                         hbuf[:, c * 256:(c + 1) * 256], ACT.Square,
                                         accum_out=small[:, 16 + c:17 + c]).then_inc(m_ss, 1)
                    act.wait_ge(m_ss, 8 * j + c + 1)
                nc.scalar.activation(small[:, 24:32], small[:, 16:24], ACT.Sqrt, bias=vec[:, 4:5], scale=1.0 / 256
                                     ).then_inc(m_rms, 1)

            mlstm_act(0, True)
            with act.Fori(1, M_HEADS) as j:
                mlstm_act(j, False)

            def squares(n, src):
                nc.scalar.activation(prob[:, 0, :], src, ACT.Square).then_inc(a_sq, 1)

            def root(n):
                act.wait_ge(a_ssum, n + 1)
                nc.scalar.activation(psS, flat(6), ACT.Sqrt, bias=vec[:, 4:5], scale=1.0 / P).then_inc(a_rms, 1)

            def exponentials(g, i):
                act.wait_ge(a_m, 8 * g + i + 1)
                nc.scalar.activation(prob[:, i % 2, :], prob[:, i % 2, :], ACT.Exp, bias=small[:, i % 2:i % 2 + 1],
                                     scale=-1.0, accum_out=small[:, 2 + i % 2:3 + i % 2]).then_inc(a_e, 1)

            def take_probs(g, i):
                act.wait_ge(a_t, 16 * g + 2 * i + 1)
                if i % 2 == 0 and i > 0:
                    act.wait_ge(a_pv, 4 * g + i // 2)
                nc.scalar.copy(pT[:, 0:4, (i % 2) * P:(i % 2 + 1) * P], ps[:, 2, :].rearrange("p (b q) -> p b q", q=P)
                               ).then_inc(a_ta, 1)

            def attention_ops(g, u):
                if u == 0:
                    act.wait_ge(a_rope, 14 * g + 7)
                    squares(2 * g + 1, kT[:])
                    root(2 * g + 1)
                if 6 <= u <= 13:
                    take_probs(g, u - 6)
                if 4 <= u <= 11:
                    exponentials(g, u - 4)

            def attention_act(h, first):
                tile0 = h * A_TILES + A_TILE
                for u in range(A_PIECES):
                    ahead((tile0 + u // PIECES, u % PIECES))
                    if first and u == 0:
                        m_square_sums(M_HEADS - 1)
                    if not first:
                        attention_ops(h - 1, u)
                    if u == 3:
                        tile_end(tile0)
                        if first:
                            act.wait_ge(m_g, 2 * M_HEADS)
                        nc.scalar.copy(vst[:], flat(0)).then_inc(a_vst, 1)
                        act.wait_ge(a_vst, h + 1)
                        act.sem_inc(proj_free, 1)
                    if u == 7:
                        tile_end(tile0 + 1)
                        if first:
                            act.wait_ge(m_y, 4 * M_HEADS)
                        else:
                            act.wait_ge(a_zg, h)
                        nc.scalar.activation(zst[:], flat(0), ACT.Silu).then_inc(a_z, 1)
                        act.wait_ge(a_z, h + 1)
                        act.sem_inc(proj_free, 1)
                    if u == 11:
                        tile_end(tile0 + 2)
                        if not first:
                            act.wait_ge(a_s, 8 * h)
                        nc.scalar.copy(qT[:], flat(0)).then_inc(a_qk_out, 1)
                        act.wait_ge(a_qk_out, 2 * h + 1)
                        act.sem_inc(proj_free, 1)
                    if u == 13:
                        if not first:
                            act.wait_ge(a_t, 16 * h - 2)
                        else:
                            act.wait_ge(m_out, 16 * M_HEADS)
                        squares(2 * h, qT[:])
                        root(2 * h)
                    if u == 15:
                        act.wait_ge(a_vtr, 2 * h + 1)
                        nc.scalar.copy(vtok[:, 0:4, :], ps[:, 2, :].rearrange("p (b d) -> p b d", d=P)
                                       ).then_inc(a_va, 1)
                        tile_end(tile0 + 3)
                        nc.scalar.copy(kT[:], flat(0)).then_inc(a_qk_out, 1)
                        act.wait_ge(a_qk_out, 2 * h + 2)
                        act.sem_inc(proj_free, 1)

            attention_act(0, True)
            with act.Fori(1, ATT_HEADS) as h:
                attention_act(h, False)
            for u in range(A_PIECES):
                attention_ops(ATT_HEADS - 1, u)
                if u == 14:
                    pass

            for kt in range(KT):
                act.wait_ge(o_in[kt % 2], 16 * (kt // 2 + 1))
                if kt == 0:
                    act.wait_ge(w_used, O_PIECE)
                nc.scalar.copy(h_hi[:, kt, :], yblk[:, kt % 2, :]).then_inc(o_hi, 1)
            for s in range(PIECES):
                ahead((O_TILE, s))
            with act.Fori(O_TILE + 1, O_TILE + O_TILES - 1) as tile:
                for s in range(PIECES):
                    ahead((tile, s))
            for s in range(PIECES - LEAD):
                ahead((O_TILE + O_TILES - 1, s))

        @block.vector
        def _(dve):
            nc.vector.memset(ones[:], 1.0).then_inc(ones_set, 1)
            dve.wait_ge(consts, 80)
            nc.vector.tensor_scalar(vec[:, 3:4], vec[:, 0:1], -float(P) ** -0.5, None, ALU.mult).then_inc(prep, 1)
            nc.vector.memset(vec[:, 4:5], EPS).then_inc(prep, 1)
            dve.wait_ge(x_rms, 1)
            nc.vector.reciprocal(xrs[:], xrs[:]).then_inc(x_rs, 1)
            dve.wait_ge(x_rs, 1)

            def low_part(kt):
                dve.wait_ge(h_hid, kt + 1)
                nc.vector.tensor_tensor(h_lo[:, kt, :], hblk[:, kt % 4, :], h_hi[:, kt, :].bitcast(F32), ALU.subtract
                                        ).then_inc(h_lod, 1)
            for kt in range(KT):
                n = KT + kt
                dve.wait_ge(x_in[n % 4], 16 * (n // 4 + 1))
                if kt >= 4:
                    dve.wait_ge(h_lod, kt - 3)
                nc.vector.scalar_tensor_tensor(hblk[:, kt % 4, :], xblk[:, kt % 4, :], ncol[:, kt:kt + 1], xrs[:],
                                               ALU.mult, ALU.mult).then_inc(h_full, 1)
                if kt >= 1:
                    low_part(kt - 1)
                if kt == KT - 3:
                    weight_lo(dve, 0, 0)
                if kt == KT - 2:
                    weight_lo(dve, 0, 1)
            low_part(KT - 1)

            def ahead(piece_at):
                tile, s = piece_at
                weight_lo(dve, tile + (s + LEAD) // PIECES, (s + LEAD) % PIECES)

            for s in range(PIECES):
                ahead((0, s))
            dve.wait_ge(h_lod, KT)
            nc.vector.memset(v1[:, :, 256:258], 1.0).then_inc(prep, 1)

            count = [0]

            def g_step(ins):
                ins.then_inc(g_dve, 1)
                count[0] += 1
                dve.wait_ge(g_dve, count[0])

            def gate_rows():
                raw, li, f, m, t, wi = gr
                dve.wait_ge(proj_free, 1)
                g_step(nc.vector.tensor_copy(li[0:32, :], raw[0:32, :]))
                g_step(nc.vector.tensor_copy(li[32:64, :], raw[32:64, ::-1]))
                g_step(nc.vector.tensor_copy(f[0:32, :], raw[64:96, :]))
                g_step(nc.vector.tensor_copy(f[32:64, :], raw[96:128, ::-1]))
                assert count[0] == GD_SPLIT
                dve.wait_ge(g_act, 3)
                g_step(nc.vector.scalar_tensor_tensor(f[0:64, :], f[0:64, :], 0.0, t[0:64, :], ALU.min, ALU.subtract))
                g_step(nc.vector.tensor_tensor_scan(out=m[0:64, :], data0=f[0:64, :], data1=li[0:64, :], initial=NEG,
                                                    op0=ALU.add, op1=ALU.max))
                g_step(nc.vector.memset(t[0:64, :], 0.0))
                for c in range(TB):
                    cols = slice(c * P, (c + 1) * P)
                    g_step(nc.vector.tensor_tensor_scan(out=raw[0:64, cols], data0=f[0:64, cols], data1=t[0:64, cols],
                                                        initial=0.0, op0=ALU.add, op1=ALU.add))
                g_step(nc.vector.tensor_tensor(f[0:64, :], li[0:64, :], raw[0:64, :], ALU.subtract))
                g_step(nc.vector.tensor_tensor(t[0:64, :], raw[0:64, :], m[0:64, :], ALU.subtract))
                g_step(nc.vector.tensor_scalar(wi[0:64, 0:P], t[0:64, 0:P], NEG, None, ALU.add))
                for c in range(1, TB):
                    g_step(nc.vector.tensor_scalar(wi[0:64, c * P:(c + 1) * P], t[0:64, c * P:(c + 1) * P],
                                                   m[0:64, c * P - 1:c * P], None, ALU.add))
                assert count[0] == GD_INTER
                g_step(nc.vector.tensor_copy(rows[0:32, :], t[0:32, :]))
                g_step(nc.vector.tensor_copy(rows[32:64, :], t[32:64, ::-1]))
                g_step(nc.vector.tensor_copy(li[0:32, :], m[0:32, :]))
                g_step(nc.vector.tensor_copy(li[32:64, :], m[32:64, ::-1]))
                g_step(nc.vector.tensor_copy(m[0:32, :], f[0:32, :]))
                g_step(nc.vector.tensor_copy(m[32:64, :], f[32:64, ::-1]))
                dve.wait_ge(g_act, 4)
                g_step(nc.vector.tensor_copy(rows[64:96, :], wi[0:32, :]))
                g_step(nc.vector.tensor_copy(rows[96:128, :], wi[32:64, ::-1]))
                assert count[0] == GD_ROWS

            def gate_cols():
                dve.wait_ge(g_pe, 1)
                for d in range(2):
                    src = ps[:, 4, :].rearrange("p (c r) -> p c r", r=64)[:, :, 32 * d:32 * d + M_HEADS]
                    g_step(nc.vector.tensor_copy(g_cols[:, :, d, :], src))

            def m_mask(j, n):
                d, i = n // TB, n % 2
                dve.wait_ge(m_x, 16 * j + n + 1)
                if n >= 2 or not isinstance(j, int) or j > 0:
                    dve.wait_ge(m_kw, 16 * j + n - 1)
                    dve.wait_ge(m_num, 16 * j + n - 1)
                    dve.wait_ge(m_ops, 16 * j + n - 1)
                nc.vector.tensor_tensor(chunkbuf[:, i, 0, :], ps[:, 6, 0:P], tri_m[:, d, :], ALU.add).then_inc(m_t, 1)

            def m_operands(j, n):
                c, d, i = chunk_of(n), n // TB, n % 2
                end = 0 if d else P - 1
                nc.vector.tensor_tensor(chunkbuf[:, i, 2, :], qT[:, c * P:(c + 1) * P], ps[:, 6, P:2 * P], ALU.mult)
                if n >= 2 or not isinstance(j, int) or j > 0:
                    dve.wait_ge(m_c, 16 * j + n - 1)
                nc.vector.tensor_copy(small[:, 8 + i:9 + i], ps[:, 6, P + end:P + end + 1])
                dve.wait_ge(m_w, 16 * j + n + 1)
                nc.vector.tensor_tensor(chunkbuf[:, i, 1, :], ps[:, 6, 2 * P:3 * P], chunkbuf[:, i, 0, :], ALU.mult
                                        ).then_inc(m_ops, 1)

            def m_results(j, n):
                c, d, i = chunk_of(n), n // TB, n % 2
                dve.wait_ge(m_upd, 16 * j + n + 1)
                after = cst[:, (n + 1) % 2, 0:MV]
                if n % TB == 0:
                    nc.vector.tensor_copy(after, ps[:, 5, 0:MV]).then_inc(m_c, 1)
                else:
                    dve.wait_ge(m_c, 16 * j + n)
                    nc.vector.scalar_tensor_tensor(after, cst[:, n % 2, 0:MV], small[:, 8 + i:9 + i], ps[:, 5, 0:MV],
                                                   ALU.mult, ALU.add).then_inc(m_c, 1)
                den = ps[:, 4, 256:257]
                nc.vector.tensor_scalar(small[:, 10:11], den, ec[:, c, d:d + 1], None, ALU.max).then_inc(m_den, 1)
                dve.wait_ge(m_den, 48 * j + 3 * n + 1)
                nc.vector.scalar_tensor_tensor(small[:, 11:12], den, -1.0, small[:, 10:11], ALU.mult, ALU.max
                                               ).then_inc(m_den, 1)
                dve.wait_ge(m_den, 48 * j + 3 * n + 2)
                nc.vector.reciprocal(small[:, 12:13], small[:, 11:12]).then_inc(m_den, 1)
                dve.wait_ge(m_den, 48 * j + 3 * n + 3)
                h_at = hbuf[:, c * 256:(c + 1) * 256]
                if d == 0:
                    nc.vector.tensor_scalar(h_at, ps[:, 4, 0:256], small[:, 12:13], None, ALU.mult).then_inc(m_h, 1)
                else:
                    if n == TB:
                        dve.wait_ge(m_h, 16 * j + n)
                    nc.vector.scalar_tensor_tensor(h_at, ps[:, 4, 0:256], small[:, 12:13], h_at, ALU.mult, ALU.add
                                                   ).then_inc(m_h, 1)

            def m_normalise(j):
                dve.wait_ge(m_rms, j + 1)
                nc.vector.reciprocal(small[:, 32:40], small[:, 24:32]).then_inc(m_rs, 1)
                dve.wait_ge(m_rs, j + 1)
                for c in range(TB):
                    nc.vector.tensor_scalar(hbuf[:, c * 256:(c + 1) * 256], hbuf[:, c * 256:(c + 1) * 256],
                                            small[:, 32 + c:33 + c], None, ALU.mult).then_inc(m_hn, 1)

            def m_outputs(j, e):
                for b in range(2):
                    dve.wait_ge(m_htr, 4 * j + 2 * e + b + 1)
                    at = gate[:, e * SEQ + b * HALF:e * SEQ + (b + 1) * HALF]
                    nc.vector.tensor_tensor(at, ps[:, 2 + b, :], at, ALU.mult).then_inc(m_y, 1)

            def mlstm_dve(j, first):
                tile0 = j * M_TILES + G_TILE
                for u in range(M_PIECES):
                    ahead((tile0 + u // PIECES, u % PIECES))
                    if first and u == 0:
                        gate_rows()
                    if first and u == 4:
                        gate_cols()
                    if not first:
                        if u == 0:
                            m_gates(j - 1, 1)
                            m_normalise(j - 1)
                        if u in (1, 2):
                            m_outputs(j - 1, u - 1)
                    if u in (4, 8):
                        half = u // 4 - 1
                        dve.wait_ge(m_vtr, 4 * j + 2 * half + 2)
                        nc.vector.tensor_copy(v1[:, 4:8, half * P:(half + 1) * P],
                                              ps[:, 3, :].rearrange("p (b d) -> p b d", d=P)).then_inc(m_vd, 1)
                    if u == 28:
                        m_gates(j, 0)
                    if u >= 16:
                        m_results(j, u - 16)
                    if 15 <= u < 31:
                        m_mask(j, u - 15)
                        m_operands(j, u - 15)

            def m_gates(j, e):
                dve.wait_ge(m_gate, 4 * j + 3 + e)
                at = gate[:, e * SEQ:(e + 1) * SEQ]
                nc.vector.scalar_tensor_tensor(at, vst[:], mw[:, e:e + 1], at, ALU.mult, ALU.mult).then_inc(m_g, 1)

            mw = small[:, 40:42]
            mlstm_dve(0, True)
            with dve.Fori(1, M_HEADS) as j:
                mlstm_dve(j, False)

            def rotate(n, qk, w, tmp):
                at = 7 * n
                dve.wait_ge(a_rms, n + 1)
                nc.vector.reciprocal(psS, psS).then_inc(a_rope, 1)
                dve.wait_ge(a_rope, at + 1)
                nc.vector.scalar_tensor_tensor(qk, qk, w, psS, ALU.mult, ALU.mult).then_inc(a_rope, 1)
                dve.wait_ge(a_rope, at + 2)
                nc.vector.memset(small[:, 48:49], 0.0)
                nc.vector.stream_shuffle(tmp[0:ROT, :], qk[0:ROT, :], mask=[(r + ROT // 2) % ROT for r in range(ROT)]
                                         ).then_inc(a_rope, 1)
                dve.wait_ge(a_rope, at + 3)
                nc.vector.tensor_tensor(tmp[0:ROT, :], tmp[0:ROT, :], sin[0:ROT, :], ALU.mult).then_inc(a_rope, 1)
                nc.vector.tensor_tensor(qk[0:ROT, :], qk[0:ROT, :], cos[0:ROT, :], ALU.mult).then_inc(a_rope, 1)
                dve.wait_ge(a_rope, at + 5)
                nc.vector.tensor_tensor(qk[0:ROT, :], qk[0:ROT, :], tmp[0:ROT, :], ALU.add).then_inc(a_rope, 2)

            def masked(g, i):
                dve.wait_ge(a_s, 8 * g + i + 1)
                if i >= 2:
                    dve.wait_ge(a_t, 16 * g + 2 * i - 2)
                nc.vector.memset(small[:, 48:49], 0.0)
                dve.wait_ge(a_out, 16)
                at = P * (TB - 1 - i)
                nc.vector.tensor_tensor_reduce(prob[:, i % 2, :], psS, amask[:, at:at + SEQ], 1.0, -3 * NEG,
                                               ALU.add, ALU.min, small[:, i % 2:i % 2 + 1]).then_inc(a_m, 1)

            def normalised(g, i):
                dve.wait_ge(a_e, 8 * g + i + 1)
                nc.vector.reciprocal(small[:, 4 + i % 2:5 + i % 2], small[:, 2 + i % 2:3 + i % 2]).then_inc(a_r, 1)
                dve.wait_ge(a_r, 8 * g + i + 1)
                nc.vector.tensor_scalar(prob[:, i % 2, :], prob[:, i % 2, :], small[:, 4 + i % 2:5 + i % 2], None,
                                        ALU.mult).then_inc(a_p, 1)

            def attention_ops(g, u):
                if u == 0:
                    rotate(2 * g + 1, kT, vec[:, 1:2], prob[:, 1, :])
                    dve.wait_ge(a_z, g + 1)
                    dve.wait_ge(a_out, 16 * (g + 1))
                    nc.vector.tensor_copy(zg[:], zst[:]).then_inc(a_zg, 1)
                if 5 <= u <= 12:
                    normalised(g, u - 5)
                if 4 <= u <= 11:
                    masked(g, u - 4)
                if 6 <= u <= 13:
                    i = u - 6
                    dve.wait_ge(a_t, 16 * g + 2 * i + 2)
                    if i % 2 == 0 and i > 0:
                        dve.wait_ge(a_pv, 4 * g + i // 2)
                    nc.vector.tensor_copy(pT[:, 4:8, (i % 2) * P:(i % 2 + 1) * P],
                                          ps[:, 3, :].rearrange("p (b q) -> p b q", q=P)).then_inc(a_td, 1)
                if u in (8, 10, 12, 14):
                    j = (u - 8) // 2
                    dve.wait_ge(a_pv, 4 * g + j + 1)
                    if j == 0:
                        dve.wait_ge(a_zg, g + 1)
                    at = zg[:, j * 256:(j + 1) * 256]
                    nc.vector.tensor_tensor(at, ps[:, 6 + j % 2, 0:256], at, ALU.mult).then_inc(a_y, 1)

            def attention_dve(h, first):
                tile0 = h * A_TILES + A_TILE
                for u in range(A_PIECES):
                    ahead((tile0 + u // PIECES, u % PIECES))
                    if first and u == 0:
                        m_gates(M_HEADS - 1, 1)
                        m_normalise(M_HEADS - 1)
                    if first and u in (1, 2):
                        m_outputs(M_HEADS - 1, u - 1)
                    if not first:
                        attention_ops(h - 1, u)
                    if u == 15:
                        dve.wait_ge(a_cs, 32 * h + 32)
                        rotate(2 * h, qT, vec[:, 3:4], prob[:, 1, :])
                        dve.wait_ge(a_vtr, 2 * h + 2)
                        nc.vector.tensor_copy(vtok[:, 4:8, :], ps[:, 3, :].rearrange("p (b d) -> p b d", d=P)
                                              ).then_inc(a_vd, 1)

            attention_dve(0, True)
            with dve.Fori(1, ATT_HEADS) as h:
                attention_dve(h, False)
            for u in range(A_PIECES):
                attention_ops(ATT_HEADS - 1, u)

            for kt in range(KT):
                dve.wait_ge(o_hi, kt + 1)
                nc.vector.tensor_tensor(h_lo[:, kt, :], yblk[:, kt % 2, :], h_hi[:, kt, :].bitcast(F32), ALU.subtract
                                        ).then_inc(o_lo, 1)

            def output(tile, i, n2, first):
                dve.wait_ge(w_used, (tile + 1) * PIECES)
                dve.wait_ge(o_x[i], 16 * (n2 + 1))
                if not first:
                    dve.wait_ge(o_out[i], 16 * n2)
                nc.vector.tensor_tensor(oblk[:, i, :], flat(0), xres[:, i, :], ALU.add).then_inc(proj_free, 1)

            for i in range(2):
                for s in range(PIECES):
                    ahead((O_TILE + i, s))
                output(O_TILE + i, i, 0, True)
            with dve.Fori(1, O_TILES // 2 - 1) as n2:
                for i in range(2):
                    for s in range(PIECES):
                        ahead((n2 * 2 + O_TILE + i, s))
                    output(n2 * 2 + O_TILE + i, i, n2, False)
            last = O_TILES // 2 - 1
            for i in range(2):
                for s in range(PIECES if i == 0 else PIECES - LEAD):
                    ahead((O_TILE + 2 * last + i, s))
                output(O_TILE + 2 * last + i, i, last, False)

        @block.gpsimd
        def _(pool):
            pool.wait_ge(consts, 80)

            nc.gpsimd.memset(small[:, 50:51], 0.0).then_inc(p_held, 1)

            def held(k):
                pool.wait_ge(p_held, k + 1)
                nc.gpsimd.tensor_tensor(small[:, 51:52], small[:, 50:51], small[:, 50:51], ALU.add
                                        ).then_inc(p_held, 1)

            def select(j, first):
                if first:
                    pool.wait_ge(g_dve, GD_COLS)
                    pool.wait_ge(g_act, 6)
                    pool.wait_ge(prep, 3)
                else:
                    pool.wait_ge(m_h, 16 * j)
                    pool.wait_ge(m_g, 2 * j)
                at = 6 * j
                n = 0
                for d in range(2):
                    for half in range(2):
                        nc.gpsimd.tensor_copy(sel[:, 2 * d + half, :],
                                              ident[:, bass.ds(j + 64 * half + 32 * d, 1)].to_broadcast([P, P])
                                              ).then_inc(m_pick, 1)
                        n += 1
                        pool.wait_ge(m_pick, at + n)
                nc.gpsimd.tensor_copy(gc[:], g_cols[:, :, :, bass.ds(j, 1)].rearrange("p c d h -> p c (d h)")
                                      ).then_inc(m_pick, 1)
                pool.wait_ge(m_pick, at + 5)
                nc.gpsimd.tensor_copy(small[:, 40:42], mcol[:, bass.ds(2 * j, 2)]).then_inc(m_pick, 1)
                pool.wait_ge(m_pick, at + 6)
                nc.gpsimd.tensor_copy(ec[:], e_cols[:, :, :, bass.ds(j, 1)].rearrange("p c d h -> p c (d h)")
                                      ).then_inc(m_sel, 1)

            def store_mlstm(j):
                pool.wait_ge(m_y, 4 * j + 4)
                if not isinstance(j, int):
                    held(j)
                pool.dma_start(y_dram[bass.ds(2 * j, 2)].rearrange("e p t -> p e t"),
                               gate.rearrange("p (e t) -> p e t", e=2)).then_inc(m_out, 16)

            select(0, True)
            with pool.Fori(1, M_HEADS) as j:
                select(j, False)
                store_mlstm(j - 1)
            store_mlstm(M_HEADS - 1)
            pool.wait_ge(m_h, 16 * M_HEADS)
            pool.dma_start(amask[:], att_mask).then_inc(a_out, 16)

            def tables():
                pool.dma_start(cos[0:ROT, :], rope[0]).then_inc(a_cs, 16)
                pool.dma_start(sin[0:ROT, :], rope[1]).then_inc(a_cs, 16)

            tables()
            with pool.Fori(1, ATT_HEADS) as h:
                pool.wait_ge(a_pv, 4 * h)
                held(2 * h + M_HEADS - 3)
                tables()
                pool.wait_ge(a_y, 4 * h)
                held(2 * h + M_HEADS - 2)
                pool.dma_start(y_dram[bass.ds(h - 1 + 2 * M_HEADS, 1)].rearrange("e p t -> p (e t)"), zg[:]
                               ).then_inc(a_out, 16)
            pool.wait_ge(a_y, 4 * ATT_HEADS)
            pool.dma_start(y_dram[2 * M_HEADS + ATT_HEADS - 1], zg[:]).then_inc(a_out, 16)

            for kt in range(KT):
                if kt == 0:
                    pool.wait_ge(a_pv, 4 * ATT_HEADS)
                    pool.wait_ge(m_out, 16 * M_HEADS)
                    pool.wait_ge(a_out, 16 * ATT_HEADS)
                if kt == KT - 1:
                    pool.wait_ge(a_out, 16 * (ATT_HEADS + 1))
                if kt >= 2:
                    pool.wait_ge(o_lo, kt - 1)
                pool.dma_start(yblk[:, kt % 2, :], y_dram[kt]).then_inc(o_in[kt % 2], 16)
            for i in range(2):
                pool.dma_start(xres[:, i, :], xT[i]).then_inc(o_x[i], 16)
            with pool.Fori(0, O_TILES // 2 - 1) as n2:
                for i in range(2):
                    pool.wait_ge(proj_free, n2 * 2 + O_TILE + i + 1)
                    held(2 * n2 + M_HEADS - 1 + 2 * (ATT_HEADS - 1) + i)
                    pool.dma_start(outT[bass.ds(2 * n2 + i, 1)].rearrange("a p t -> p (a t)"), oblk[:, i, :]
                                   ).then_inc(o_out[i], 16)
                    pool.dma_start(xres[:, i, :], xT[bass.ds(2 * n2 + 2 + i, 1)].rearrange("a p t -> p (a t)")
                                   ).then_inc(o_x[i], 16)
            for i in range(2):
                pool.wait_ge(proj_free, O_TILE + O_TILES - 2 + i + 1)
                pool.dma_start(outT[O_TILES - 2 + i], oblk[:, i, :]).then_inc(o_out[i], 16)
            for i in range(2):
                pool.wait_ge(o_out[i], 16 * (O_TILES // 2))


GD_SPLIT = 4
GD_INTER = GD_SPLIT + 3 + TB + 2 + TB
GD_ROWS = GD_INTER + 8
GD_COLS = GD_ROWS + 2


def shape_constants():
    pos = np.arange(SEQ, dtype=np.float32)
    inv = (500000.0 ** (-np.arange(0, ROT, 2, dtype=np.float32) / ROT)).astype(np.float32)
    ang = (pos[:, None] * inv[None, :]).astype(np.float32).T
    c, s = np.cos(ang), np.sin(ang)
    rope = np.stack([np.concatenate([c, c]), np.concatenate([-s, s])]).astype(np.float32)
    rel = np.arange(MASK_W)[None, :] - np.arange(P)[:, None] - P * (TB - 1)
    n = np.zeros(rel.shape)
    for window, dil in ((128, 1), (512, 4), (2048, 16)):
        n += (rel % dil == 0) & (np.abs(rel) // dil <= window // (2 * dil))
    table = np.where(n > 0, -np.log(np.maximum(n, 1)), -NEG).astype(np.float32)
    s_, t_ = np.arange(P)[:, None], np.arange(P)[None, :]
    tri = np.stack([np.where(s_ <= t_, 0.0, NEG), np.where(s_ >= t_, 0.0, NEG)], axis=1).astype(np.float32)
    return rope, table, np.eye(P, dtype=np.float32), tri


def weight_pieces(w):
    n = w.shape[1] // P
    return w.reshape(PIECES, KP, P, n, P).transpose(3, 0, 2, 1, 4).reshape(n * PIECES, P, KP * P)


def kernel(x, norm_w, w_in, b_gates, q_norm_w, k_norm_w, m_norm_w, w_out):
    import numpy as _np
    import concourse.bacc as _bacc
    from concourse import mybir as _mybir
    from concourse.bass_utils import run_bass_kernel_spmd as _run

    x, norm_w, w_in, b_gates, q_norm_w, k_norm_w, m_norm_w, w_out = (
        _np.asarray(a) for a in (x, norm_w, w_in, b_gates, q_norm_w, k_norm_w, m_norm_w, w_out))
    w = w_in[0]
    qa, ka, va, za, qm, km, vm, om, zm, g = _np.split(
        w, _np.cumsum([1024, 1024, 1024, 1024, 512, 512, 1024, 1024, 1024]).tolist(), axis=1)
    gates = _np.zeros((D_MODEL, P), w.dtype)
    bias = _np.zeros(P, w.dtype)
    for at, k in ((0, 0), (64, 1), (32, 2), (96, 3)):
        gates[:, at:at + M_HEADS] = g[:, k * M_HEADS:(k + 1) * M_HEADS]
        bias[at:at + M_HEADS] = b_gates[0, k * M_HEADS:(k + 1) * M_HEADS]
    cols = [gates]
    for j in range(M_HEADS):
        cols += [vm[:, 256 * j:256 * (j + 1)], km[:, P * j:P * (j + 1)], qm[:, P * j:P * (j + 1)],
                 om[:, 256 * j:256 * (j + 1)], zm[:, 256 * j:256 * (j + 1)]]
    for h in range(ATT_HEADS):
        cols += [a[:, P * h:P * (h + 1)] for a in (va, za, qa, ka)]
    wo = _np.concatenate([w_out[0][1024:], w_out[0][:1024]], axis=0)
    w_all = _np.ascontiguousarray(weight_pieces(_np.concatenate(cols + [wo], axis=1)))
    rope, table, eye, tri = shape_constants()
    vecs = _np.zeros((P, 8), w.dtype)
    vecs[:, 0], vecs[:, 1], vecs[:, 2] = q_norm_w[0], k_norm_w[0], bias
    arrays = {
        "xT_dram": _np.ascontiguousarray(x[0].T).reshape(KT, P, SEQ),
        "w_all_dram": w_all,
        "vecs_dram": vecs,
        "norm_cols_dram": _np.ascontiguousarray(norm_w[0].reshape(KT, P).T),
        "m_cols_dram": _np.ascontiguousarray(m_norm_w[0].reshape(8, P).T),
        "att_mask_dram": table,
        "rope_dram": rope,
        "eye_dram": eye,
        "tri_dram": tri,
    }
    nc = _bacc.Bacc("TRN2", target_bir_lowering=False, num_devices=1)
    args = [nc.dram_tensor(n, a.shape, _mybir.dt.float32, kind="ExternalInput").ap() for n, a in arrays.items()]
    y_dram = nc.dram_tensor("y_dram", (KT, P, SEQ), _mybir.dt.float32, kind="Internal").ap()
    outT = nc.dram_tensor("outT_dram", (O_TILES, P, SEQ), _mybir.dt.float32, kind="ExternalOutput").ap()
    build_program(nc, *args, y_dram, outT)
    r = _run(nc, [arrays], core_ids=[0])
    return _np.ascontiguousarray(r.results[0]["outT_dram"].reshape(D_MODEL, SEQ).T).reshape(1, SEQ, D_MODEL)
```

```python
from contextlib import ExitStack

import numpy as np

import concourse.bass as bass
from concourse import mybir

F32 = mybir.dt.float32
F32R = mybir.dt.float32r
ALU = mybir.AluOpType
ACT = mybir.ActivationFunctionType

P = 128
D_MODEL = 2048
SEQ = 1024
KT = D_MODEL // P
HALF = 512
TB = SEQ // P
PIECES = 4
KP = KT // PIECES
LEAD = 3

ATT_HEADS = 8
ROT = 32
M_HEADS = 4
A_TILES = 3
M_TILES = 8
A_PIECES = A_TILES * PIECES
M_PIECES = M_TILES * PIECES
G_PIECE = PIECES
A_PIECE = G_PIECE + M_HEADS * M_PIECES
Z_PIECE = A_PIECE + ATT_HEADS * A_PIECES
O_PIECE = Z_PIECE + ATT_HEADS * PIECES
O_TILES = D_MODEL // P
N_PIECE = O_PIECE + O_TILES * PIECES
G_TILE, A_TILE, Z_TILE, O_TILE = (n // PIECES for n in (G_PIECE, A_PIECE, Z_PIECE, O_PIECE))

EPS = 1e-6
NEG = -1e30
V1 = 258
MV = 257
STEPS = 2 * TB
CLASSES = 4
EDGE = 16
KEYS = 4 * P + CLASSES * EDGE + P
MASK_A = (2 * CLASSES - 1) * P
MASK_B = KEYS - 4 * P
FIRST_SCORES, FIRST_TURN = 7, 9


def chunk_of(n):
    return n if n < TB else STEPS - 1 - n


def build_program(nc, xT, w_all, vecs, norm_cols, m_cols, att_mask, rope, eye, tri, y_dram, outT):
    with ExitStack() as ctx:
        def sb(name, shape, dt=F32):
            return ctx.enter_context(nc.sbuf_tensor(name, shape, dt))

        def sem(name):
            return ctx.enter_context(nc.semaphore(name))

        h_hi = sb("h_hi", [P, KT, SEQ], F32R)
        h_lo = sb("h_lo", [P, KT, SEQ], F32R)
        h_lo_end = nc.sbuf_base
        w_raw = sb("w_raw", [P, PIECES, KP * P])
        w_hi = sb("w_hi", [P, PIECES, KP * P], F32R)
        w_lo = sb("w_lo", [P, PIECES, KP * P], F32R)
        ident = sb("ident", [P, P])
        ones = sb("ones", [P, P])
        vec = sb("vec", [P, 8])
        ncol = sb("ncol", [P, KT])
        mcol = sb("mcol", [P, 8])
        tri_m = sb("tri_m", [P, 2, P])
        small = sb("small", [P, 64])
        g_cols = sb("g_cols", [P, TB, 2, M_HEADS])
        e_cols = sb("e_cols", [P, TB, 2, M_HEADS])
        a_cols = sb("a_cols", [P, TB, 4, M_HEADS])
        A_FL = 12672
        arena = sb("arena", [P, A_FL])

        def view(at, n):
            return arena[:, at:at + n]

        qT, kT = view(0, 1024), view(1024, 1024)
        hbuf = view(2048, 2048)
        gate = view(4096, 2048)
        vst = view(6144, 1024)
        v1 = view(7168, TB * V1).rearrange("p (c e) -> p c e", e=V1)
        rows = view(9232, 1024)
        chunkbuf = view(10256, 2 * 4 * P).rearrange("p (i k t) -> p i k t", i=2, k=4)
        cst = view(11280, 2 * V1).rearrange("p (i e) -> p i e", e=V1)
        ac = view(11796, 4 * TB).rearrange("p (c k d) -> p c k d", k=2, d=2)
        gc = view(12308, 2 * TB).rearrange("p (c d) -> p c d", d=2)
        ec = view(12324, 2 * TB).rearrange("p (c d) -> p c d", d=2)
        a_v = view(0, 1024)
        a_q, a_k = view(1024, 1024), view(2048, 1024)
        prob = view(3072, 2048).rearrange("p (i k) -> p i k", i=2)
        mask_a = view(5120, MASK_A)
        mask_b = view(5120 + MASK_A, 8 * MASK_B).rearrange("p (i k) -> p i k", i=8)
        ystage = view(7552, 1024)
        vtok = view(8576, 1024).rearrange("p (b d) -> p b d", d=P)
        vedge = view(9600, 256).rearrange("p (h d) -> p h d", d=P)
        pT = view(9856, 6 * 256).rearrange("p (b q) -> p b q", b=6)
        cos, sin = view(9856, 1024), view(10880, 1024)
        vcut = view(11904, 2 * CLASSES * EDGE).rearrange("p (e r n) -> p e r n", e=2, r=CLASSES)
        zs = view(0, 8 * SEQ)
        yring = view(8576, 4 * SEQ).rearrange("p (i t) -> p i t", i=4)
        gr = [view(2048 + 1024 * i, 1024) for i in range(4)] + [qT, kT]
        x_raw = nc.alloc_sbuf_tensor_at("x_raw", [P, KT, SEQ], F32, offset=h_lo_end - KT * SEQ * 4)
        hblk = view(4096, 4 * SEQ).rearrange("p (i t) -> p i t", i=4)
        xrs = view(8192, 1024)
        oblk = view(0, 2 * SEQ).rearrange("p (i t) -> p i t", i=2)
        xres = view(2048, 2 * SEQ).rearrange("p (i t) -> p i t", i=2)

        ps = ctx.enter_context(nc.psum_tensor("ps", [P, 8, HALF], F32))
        psP = ps[:, 0:2, :]
        psS = ps[:, 4:6, :].rearrange("p b k -> p (b k)")

        def by_class(row):
            return row.rearrange("p (r n) -> p r n", r=CLASSES)

        def flat(b):
            return ps[:, b:b + 2, :].rearrange("p b k -> p (b k)")

        w_landed = [sem(f"w_landed{i}") for i in range(PIECES)]
        w_hi_done = sem("w_hi_done")
        w_lo_done = sem("w_lo_done")
        w_used = sem("w_used")
        half_done = sem("half_done")
        proj_free = sem("proj_free")
        consts = sem("consts")
        ones_set = sem("ones_set")
        x_in = [sem(f"x_in{i}") for i in range(KT)]
        x_sq = sem("x_sq")
        x_sum = sem("x_sum")
        x_rms = sem("x_rms")
        x_rs = sem("x_rs")
        h_full = sem("h_full")
        h_hid = sem("h_hid")
        h_lod = sem("h_lod")
        prep = sem("prep")
        g_act = sem("g_act")
        g_dve = sem("g_dve")
        g_pe = sem("g_pe")
        m_sel = sem("m_sel")
        m_pick = sem("m_pick")
        m_vtr = sem("m_vtr")
        m_va = sem("m_va")
        m_vd = sem("m_vd")
        m_x = sem("m_x")
        m_t = sem("m_t")
        m_w = sem("m_w")
        m_ops = sem("m_ops")
        m_kw = sem("m_kw")
        m_num = sem("m_num")
        m_upd = sem("m_upd")
        m_c = sem("m_c")
        m_den = sem("m_den")
        m_h = sem("m_h")
        m_g = sem("m_g")
        m_ss = sem("m_ss")
        m_rms = sem("m_rms")
        m_rs = sem("m_rs")
        m_hn = sem("m_hn")
        m_htr = sem("m_htr")
        m_y = sem("m_y")
        m_out = sem("m_out")
        p_held = sem("p_held")
        a_sq = sem("a_sq")
        a_ssum = sem("a_ssum")
        a_rms = sem("a_rms")
        a_rs = sem("a_rs")
        a_bc = sem("a_bc")
        a_rope = sem("a_rope")
        a_cs = sem("a_cs")
        a_s = sem("a_s")
        a_mh = sem("a_mh")
        a_m = sem("a_m")
        a_e = sem("a_e")
        a_r = sem("a_r")
        a_p = sem("a_p")
        a_t = sem("a_t")
        a_ta = sem("a_ta")
        a_td = sem("a_td")
        a_pv = sem("a_pv")
        a_y = sem("a_y")
        a_vcut = sem("a_vcut")
        a_vtr = sem("a_vtr")
        a_va = sem("a_va")
        a_vd = sem("a_vd")
        a_out = sem("a_out")
        a_ve = sem("a_ve")
        z_in = [sem(f"z_in{i}") for i in range(4)]
        z_y = sem("z_y")
        o_hi = sem("o_hi")
        o_lo = sem("o_lo")
        o_x = [sem(f"o_x{i}") for i in range(2)]
        o_done = sem("o_done")
        o_out = [sem(f"o_out{i}") for i in range(2)]

        block = ctx.enter_context(nc.Block())

        @block.sync
        def _(sp):
            sp.dma_start(vec[:], vecs).then_inc(consts, 16)
            sp.dma_start(ncol[:], norm_cols).then_inc(consts, 16)
            sp.dma_start(mcol[:], m_cols).then_inc(consts, 16)
            sp.dma_start(ident[:], eye).then_inc(consts, 16)
            sp.dma_start(tri_m[:], tri).then_inc(consts, 16)
            for kt in range(KT):
                sp.dma_start(x_raw[:, kt, :], xT[kt]).then_inc(x_in[kt], 16)
                if kt < PIECES:
                    sp.dma_start(w_raw[:, kt, :], w_all[kt]).then_inc(w_landed[kt], 16)
            with sp.Fori(1, N_PIECE // PIECES) as tile:
                for s in range(PIECES):
                    sp.wait_ge(w_lo_done, (tile - 1) * PIECES + s + 1)
                    sp.dma_start(w_raw[:, s, :], w_all[bass.ds(tile * PIECES + s, 1)].rearrange("a p n -> p (a n)")
                                 ).then_inc(w_landed[s], 16)

        def weight_hi(act, tile, s):
            act.wait_ge(w_landed[s], (tile + 1) * 16)
            if not (isinstance(tile, int) and tile == 0):
                act.wait_ge(w_used, (tile - 1) * PIECES + s + 1)
            nc.scalar.copy(w_hi[:, s, :], w_raw[:, s, :]).then_inc(w_hi_done, 1)

        def weight_lo(dve, tile, s):
            dve.wait_ge(w_hi_done, tile * PIECES + s + 1)
            nc.vector.tensor_tensor(w_lo[:, s, :], w_raw[:, s, :], w_hi[:, s, :].bitcast(F32), ALU.subtract
                                    ).then_inc(w_lo_done, 1)

        def piece(pe, tile, s, between=None, per_block=None):
            start = isinstance(tile, int) and tile == 0
            pe.wait_ge(w_lo_done, tile * PIECES + s + 1)
            for i in range(2):
                if s == 0 and not start:
                    pe.wait_ge(proj_free, 2 * tile - 1 + i)
                for j in range(KP):
                    kt = s * KP + j
                    if per_block is not None and i == 0:
                        per_block(kt)
                    hi = w_hi[:, s, j * P:(j + 1) * P]
                    lo = w_lo[:, s, j * P:(j + 1) * P]
                    cols = slice(i * HALF, (i + 1) * HALF)
                    nc.tensor.matmul(psP[:, i, :], hi, h_hi[:, kt, cols], start=kt == 0, stop=False)
                    nc.tensor.matmul(psP[:, i, :], hi, h_lo[:, kt, cols], start=False, stop=False)
                    mm = nc.tensor.matmul(psP[:, i, :], lo, h_hi[:, kt, cols], start=False, stop=kt == KT - 1)
                if i == 0 and s == PIECES - 1:
                    mm.then_inc(half_done, 1)
                if i == 1:
                    mm.then_inc(w_used, 1)
                if between is not None:
                    between(i)

        def read_out(eng, tile, emit):
            eng.wait_ge(half_done, tile + 1)
            emit(0).then_inc(proj_free, 1)
            eng.wait_ge(w_used, (tile + 1) * PIECES)
            emit(1).then_inc(proj_free, 1)

        def tile_out(tile):
            return 2 * tile + 2

        @block.tensor
        def _(pe):
            pe.wait_ge(ones_set, 1)
            pe.wait_ge(consts, 80)
            for kt in range(KT):
                pe.wait_ge(x_sq, kt + 1)
                for i in range(2):
                    mm = nc.tensor.matmul(ps[:, 6 + i, :], ones[:], hblk[:, kt % 4, i * HALF:(i + 1) * HALF],
                                          start=kt == 0, stop=kt == KT - 1)
                mm.then_inc(x_sum, 1)

            def transposes(src, bank, n, done):
                for b in range(n):
                    t = nc.tensor.transpose(ps[:, bank + b // 4, (b % 4) * P:(b % 4 + 1) * P], src(b), ident[:])
                    if b % 4 == 3:
                        t.then_inc(done, 1)

            def on_all_partitions(out, column):
                return nc.tensor.transpose(out, column.to_broadcast([P, P]), ident[:])

            def block_made(kt):
                pe.wait_ge(h_lod, kt + 1)
            for s in range(PIECES):
                piece(pe, 0, s, per_block=block_made)

            def gate_columns():
                pe.wait_ge(g_dve, GD_ROWS)
                for b in range(2 * TB):
                    src = (gr[3] if b < TB else gr[1])[0:64, (b % TB) * P:(b % TB + 1) * P]
                    nc.tensor.transpose(ps[:, 4 + b // TB, (b % TB) * 64:(b % TB + 1) * 64], src, ident[0:64, 0:64])
                for b in range(TB):
                    t = nc.tensor.transpose(flat(6)[:, b * P:(b + 1) * P], rows[:, b * P:(b + 1) * P], ident[:])
                t.then_inc(g_pe, 1)

            def step_inputs(j, n):
                c, d = chunk_of(n), n // TB
                cols = slice(c * P, (c + 1) * P)
                if n == 0:
                    pe.wait_ge(m_sel, j + 1)
                    pe.wait_ge(proj_free, tile_out(j * M_TILES + G_TILE + 3))
                if n > 0 or not isinstance(j, int) or j > 0:
                    pe.wait_ge(m_ops, 16 * j + n)
                    pe.wait_ge(m_kw, 16 * j + n)
                on_all_partitions(ps[:, 6, 0:P], ac[:, c, 0, d:d + 1])
                on_all_partitions(ps[:, 6, P:2 * P], ac[:, c, 1, d:d + 1])
                nc.tensor.matmul(ps[:, 6, 2 * P:3 * P], kT[:, cols], qT[:, cols], start=True, stop=True)
                nc.tensor.transpose(ps[:, 7, 0:P], kT[:, cols], ident[:]).then_inc(m_x, 1)

            def step_products(j, n):
                c, i = chunk_of(n), n % 2
                first = n % TB == 0
                pe.wait_ge(m_ops, 16 * j + n + 1)
                if n == 0:
                    pe.wait_ge(m_va, 2 * j + 2)
                    pe.wait_ge(m_vd, 2 * j + 2)
                if n > 0 or not isinstance(j, int) or j > 0:
                    pe.wait_ge(m_h, 16 * j + n)
                mm = nc.tensor.matmul(ps[:, 4, 0:MV], chunkbuf[:, i, 1, :], v1[:, c, 0:MV], start=True, stop=first)
                if not first:
                    pe.wait_ge(m_c, 16 * j + n)
                    mm = nc.tensor.matmul(ps[:, 4, 0:MV], chunkbuf[:, i, 2, :], cst[:, n % 2, 0:MV],
                                          start=False, stop=True)
                mm.then_inc(m_num, 1)
                pe.wait_ge(m_kw, 16 * j + n + 1)
                if first and (n > 0 or not isinstance(j, int) or j > 0):
                    pe.wait_ge(m_c, 16 * j + n)
                nc.tensor.matmul(ps[:, 5, 0:MV], chunkbuf[:, i, 3, :], v1[:, c, 0:MV], start=True, stop=True
                                 ).then_inc(m_upd, 1)

            def m_value_transposes(j, half):
                pe.wait_ge(proj_free, tile_out(j * M_TILES + G_TILE + half))
                if half == 1:
                    pe.wait_ge(m_va, 2 * j + 1)
                    pe.wait_ge(m_vd, 2 * j + 1)
                elif not (isinstance(j, int) and j == 0):
                    pe.wait_ge(m_y, 4 * j)
                transposes(lambda b: vst[:, b * P:(b + 1) * P], 2, TB, m_vtr)

            def m_output_transposes(j, e):
                pe.wait_ge(m_hn, 8 * j + 8)
                if e == 1:
                    pe.wait_ge(m_y, 4 * j + 2)
                transposes(lambda b: hbuf[:, b * 256 + e * P:b * 256 + (e + 1) * P], 2, TB, m_htr)

            def mlstm_pe(j, first):
                for u in range(M_PIECES):
                    piece(pe, j * M_TILES + G_TILE + u // PIECES, u % PIECES)
                    if first and u == 4:
                        gate_columns()
                    if not first and u in (1, 2):
                        m_output_transposes(j - 1, u - 1)
                    if u in (4, 8):
                        m_value_transposes(j, u // 4 - 1)
                    if u >= 16:
                        step_products(j, u - 16)
                    if 15 <= u < 31:
                        step_inputs(j, u - 15)

            mlstm_pe(0, True)
            with pe.Fori(1, M_HEADS) as j:
                mlstm_pe(j, False)

            def square_sums(n):
                pe.wait_ge(a_sq, n + 1)
                for b in range(TB):
                    mm = nc.tensor.matmul(ps[:, 5, b:b + 1], prob[:, 0, b * P:(b + 1) * P], ones[:, 0:1],
                                          start=True, stop=True)
                mm.then_inc(a_ssum, 1)

            def spread(n):
                pe.wait_ge(a_rs, n + 1)
                for b in range(TB):
                    t = on_all_partitions(flat(6)[:, b * P:(b + 1) * P], small[:, 24 + b:25 + b])
                t.then_inc(a_bc, 1)

            def scores(g, i):
                h, c = divmod(i, CLASSES)
                if i == 0:
                    pe.wait_ge(a_rope, 10 * g + 10)
                else:
                    pe.wait_ge(a_m, 8 * g + i)
                q = a_q[:, c * 256 + h * P:c * 256 + (h + 1) * P]
                edge = P if h == 0 else P - EDGE
                nc.tensor.matmul(ps[:, 4, :], q, by_class(a_k)[:, :, h * P:(h + 1) * P], start=True, stop=True)
                nc.tensor.matmul(ps[:, 5, 0:CLASSES * EDGE], q, by_class(a_k)[:, :, edge:edge + EDGE],
                                 start=True, stop=True)
                nc.tensor.matmul(ps[:, 5, CLASSES * EDGE:MASK_B], q,
                                 a_k[:, c * 256 + (1 - h) * P:c * 256 + (2 - h) * P], start=True, stop=True
                                 ).then_inc(a_s, 1)

            def prob_transposes(g, i):
                pe.wait_ge(a_p, 8 * g + i + 1)
                if i == 0:
                    pe.wait_ge(a_va, g + 1)
                    pe.wait_ge(a_vd, g + 1)
                else:
                    pe.wait_ge(a_ta, 8 * g + i)
                    pe.wait_ge(a_td, 8 * g + i)
                transposes(lambda b: prob[:, i % 2, b * P:(b + 1) * P], 2, 4, a_t)
                nc.tensor.transpose(ps[:, 3, 0:P], prob[:, i % 2, KEYS - P:KEYS], ident[:])
                nc.tensor.transpose(ps[0:CLASSES * EDGE, 3, P:2 * P], prob[:, i % 2, 4 * P:KEYS - P], ident[:]
                                    ).then_inc(a_t, 1)

            def values(g, j):
                h, c = j // 2, 2 * (j % 2)
                pe.wait_ge(a_ta, 8 * g + 2 * j + 2)
                pe.wait_ge(a_td, 8 * g + 2 * j + 2)
                if j >= 2:
                    pe.wait_ge(a_y, 4 * g + j - 1)
                out = ps[:, 6 + j % 2, 0:256]
                for b in range(4):
                    nc.tensor.matmul(out, vtok[:, 4 * h + b, :], pT[:, b, :], start=b == 0, stop=False)
                for t in range(2):
                    nc.tensor.matmul(out[:, t * P:(t + 1) * P], vtok[:, 4 * (1 - h) + c + t, :],
                                     pT[:, 4, t * P:(t + 1) * P], start=False, stop=False, skip_group_check=True)
                nc.tensor.matmul(out, vedge[0:CLASSES * EDGE, h, :], pT[0:CLASSES * EDGE, 5, :], start=False, stop=True
                                 ).then_inc(a_pv, 1)

            def value_transposes(h):
                pe.wait_ge(proj_free, tile_out(h * A_TILES + A_TILE))
                if not (isinstance(h, int) and h == 0):
                    pe.wait_ge(a_ta, 8 * h)
                    pe.wait_ge(a_td, 8 * h)
                pe.wait_ge(a_vcut, h + 1)
                transposes(lambda b: a_v[:, (b % 4) * 256 + (b // 4) * P:(b % 4) * 256 + (b // 4 + 1) * P], 2, TB, a_vtr)
                for half in range(2):
                    t = nc.tensor.transpose(ps[0:CLASSES * EDGE, 4, half * P:(half + 1) * P],
                                            vcut[:, 1 - half].rearrange("p r n -> p (r n)"), ident[:])
                t.then_inc(a_vtr, 1)

            def attention_units(g, x):
                if x == 1:
                    square_sums(2 * g + 1)
                if x == 2:
                    spread(2 * g + 1)
                i = x - FIRST_TURN
                if i >= 2 and i % 2 == 0 and i <= 8:
                    values(g, i // 2 - 1)
                if 0 <= i < 8:
                    prob_transposes(g, i)
                if 0 <= x - FIRST_SCORES < 8:
                    scores(g, x - FIRST_SCORES)

            def attention_pe(h, first):
                def unit(x):
                    if first and x in (3, 5):
                        m_output_transposes(M_HEADS - 1, (x - 3) // 2)
                    if not first:
                        attention_units(h - 1, x)
                    if x == 17:
                        if not first:
                            pe.wait_ge(a_m, 8 * h)
                        square_sums(2 * h)
                    if x == 18:
                        value_transposes(h)
                    if x == 19:
                        if not first:
                            pe.wait_ge(a_y, 4 * h)
                        spread(2 * h)
                for u in range(A_PIECES):
                    piece(pe, h * A_TILES + A_TILE + u // PIECES, u % PIECES, lambda i: unit(2 * u + i))

            attention_pe(0, True)
            with pe.Fori(1, ATT_HEADS) as h:
                attention_pe(h, False)

            for u in range(A_PIECES):
                piece(pe, Z_TILE + u // PIECES, u % PIECES, lambda i: attention_units(ATT_HEADS - 1, 2 * u + i))
            with pe.Fori(Z_TILE + A_TILES, O_TILE) as tile:
                for s in range(PIECES):
                    piece(pe, tile, s)

            def y_made(kt):
                pe.wait_ge(o_lo, kt + 1)
            for s in range(PIECES):
                piece(pe, O_TILE, s, per_block=y_made)
            with pe.Fori(O_TILE + 1, O_TILE + O_TILES) as tile:
                for s in range(PIECES):
                    piece(pe, tile, s)

        GA_BIAS = 1
        @block.scalar
        def _(act):
            act.wait_ge(prep, 2)
            for kt in range(KT):
                act.wait_ge(x_in[kt], 16)
                if kt >= 4:
                    act.wait_ge(x_sum, kt - 3)
                nc.scalar.activation(hblk[:, kt % 4, :], x_raw[:, kt, :], ACT.Square).then_inc(x_sq, 1)
            for s in range(LEAD):
                weight_hi(act, 0, s)
            act.wait_ge(x_sum, KT)
            nc.scalar.activation(xrs[:], flat(6), ACT.Sqrt, bias=vec[:, 4:5], scale=1.0 / D_MODEL).then_inc(x_rms, 1)
            for kt in range(KT):
                act.wait_ge(h_full, kt + 1)
                nc.scalar.copy(h_hi[:, kt, :], hblk[:, kt % 4, :]).then_inc(h_hid, 1)

            def ahead(piece_at):
                tile, s = piece_at
                weight_hi(act, tile + (s + LEAD) // PIECES, (s + LEAD) % PIECES)

            def halves(out, func=ACT.Copy, scale=1.0):
                return lambda i: nc.scalar.activation(out[:, i * HALF:(i + 1) * HALF], psP[:, i, :], func, scale=scale)

            def halves_by_class(out):
                return lambda i: nc.scalar.copy(by_class(out)[:, :, i * P:(i + 1) * P],
                                                psP[:, i, :].rearrange("p (n r) -> p r n", r=CLASSES))

            for s in range(PIECES):
                ahead((0, s))
            read_out(act, 0, lambda i: nc.scalar.activation(gr[0][:, i * HALF:(i + 1) * HALF], psP[:, i, :],
                                                            ACT.Identity, bias=vec[:, 2:3]))

            def gate_rows():
                act.wait_ge(g_dve, GD_SPLIT)
                nc.scalar.activation(gr[4][0:64, :], gr[2][0:64, :], ACT.Abs).then_inc(g_act, 1)
                act.wait_ge(g_act, 1)
                nc.scalar.activation(gr[4][0:64, :], gr[4][0:64, :], ACT.Exp, scale=-1.0).then_inc(g_act, 1)
                act.wait_ge(g_act, 2)
                nc.scalar.activation(gr[4][0:64, :], gr[4][0:64, :], ACT.Ln, bias=1.0).then_inc(g_act, 1)
                act.wait_ge(g_dve, GD_INTER)
                nc.scalar.activation(gr[5][0:64, :], gr[5][0:64, :], ACT.Exp).then_inc(g_act, 1)

            def gate_cols():
                act.wait_ge(g_pe, 1)
                for d in range(2):
                    src = ps[:, 5, :].rearrange("p (c r) -> p c r", r=64)[:, :, 32 * d:32 * d + M_HEADS]
                    nc.scalar.activation(e_cols[:, :, d, :], src, ACT.Exp, scale=-1.0).then_inc(g_act, 1)

            def m_step(j, n):
                c, d, i = chunk_of(n), n // TB, n % 2
                act.wait_ge(m_t, 16 * j + n + 1)
                if n >= 2 or not isinstance(j, int) or j > 0:
                    act.wait_ge(m_upd, 16 * j + n - 1)
                nc.scalar.activation(chunkbuf[:, i, 0, :], chunkbuf[:, i, 0, :], ACT.Exp, bias=gc[:, c, d:d + 1]
                                     ).then_inc(m_w, 1)
                act.wait_ge(m_w, 16 * j + n + 1)
                end = 0 if d else P - 1
                nc.scalar.activation(chunkbuf[:, i, 3, :], ps[:, 7, 0:P], ACT.Copy,
                                     scale=chunkbuf[:, i, 0, end:end + 1]).then_inc(m_kw, 1)

            def mlstm_act(j, first):
                tile0 = j * M_TILES + G_TILE
                for u in range(M_PIECES):
                    ahead((tile0 + u // PIECES, u % PIECES))
                    if first and u == 0:
                        gate_rows()
                    if first and u == 4:
                        gate_cols()
                    if not first and u == 0:
                        m_square_sums(j - 1)
                    if u == 3:
                        if not first:
                            act.wait_ge(m_g, 2 * j)
                        read_out(act, tile0, halves(vst))
                    if u in (4, 8):
                        half = u // 4 - 1
                        act.wait_ge(m_vtr, 4 * j + 2 * half + 1)
                        nc.scalar.copy(v1[:, 0:4, half * P:(half + 1) * P], ps[:, 2, :].rearrange("p (b d) -> p b d", d=P)
                                       ).then_inc(m_va, 1)
                    if u == 7:
                        act.wait_ge(m_vtr, 4 * j + 2)
                        read_out(act, tile0 + 1, halves(vst))
                    if u == 11:
                        if first:
                            act.wait_ge(g_pe, 1)
                        read_out(act, tile0 + 2, halves(kT, scale=float(P) ** -0.5))
                    if u == 15:
                        read_out(act, tile0 + 3, halves(qT))
                    if u in (19, 23):
                        e = u // 4 - 4
                        if not first:
                            act.wait_ge(m_out, 16 * j)
                        read_out(act, tile0 + 4 + e, halves(gate[:, e * SEQ:(e + 1) * SEQ], ACT.Sigmoid))
                    if u in (27, 31):
                        e = u // 4 - 6
                        if e == 0:
                            act.wait_ge(m_vtr, 4 * j + 4)
                        else:
                            act.wait_ge(m_g, 2 * j + 1)
                        read_out(act, tile0 + 6 + e, halves(vst, ACT.Silu))
                    if 15 <= u < 31:
                        m_step(j, u - 15)

            def m_square_sums(j):
                for c in range(TB):
                    if c == 0:
                        act.wait_ge(m_h, 16 * j + 16)
                    nc.scalar.activation(chunkbuf[:, 0, 0:2, :].rearrange("p k t -> p (k t)"),
                                         hbuf[:, c * 256:(c + 1) * 256], ACT.Square,
                                         accum_out=small[:, 16 + c:17 + c]).then_inc(m_ss, 1)
                    act.wait_ge(m_ss, 8 * j + c + 1)
                nc.scalar.activation(small[:, 24:32], small[:, 16:24], ACT.Sqrt, bias=vec[:, 4:5], scale=1.0 / 256
                                     ).then_inc(m_rms, 1)

            mlstm_act(0, True)
            with act.Fori(1, M_HEADS) as j:
                mlstm_act(j, False)

            def squares(n, src):
                nc.scalar.activation(prob[:, 0, :], src, ACT.Square).then_inc(a_sq, 1)

            def root(n):
                act.wait_ge(a_ssum, n + 1)
                nc.scalar.activation(small[:, 16:24], ps[:, 5, 0:TB], ACT.Sqrt, bias=vec[:, 4:5], scale=1.0 / P
                                     ).then_inc(a_rms, 1)

            def exponentials(g, i):
                act.wait_ge(a_m, 8 * g + i + 1)
                nc.scalar.activation(prob[:, i % 2, 0:KEYS], prob[:, i % 2, 0:KEYS], ACT.Exp,
                                     bias=small[:, i % 2:i % 2 + 1], scale=-1.0,
                                     accum_out=small[:, 2 + i % 2:3 + i % 2]).then_inc(a_e, 1)

            def take_probs(g, i):
                act.wait_ge(a_t, 16 * g + 2 * i + 1)
                if i == 0:
                    act.wait_ge(a_rope, 10 * g + 10)
                if i % 2 == 0 and i > 0:
                    act.wait_ge(a_pv, 4 * g + i // 2)
                nc.scalar.copy(pT[:, 0:4, (i % 2) * P:(i % 2 + 1) * P], ps[:, 2, :].rearrange("p (b q) -> p b q", q=P)
                               ).then_inc(a_ta, 1)

            def attention_ops(g, x):
                if x == 0:
                    act.wait_ge(a_ssum, 2 * g + 1)
                    act.wait_ge(proj_free, tile_out(g * A_TILES + A_TILE + 2))
                    squares(2 * g + 1, a_k[:])
                if x == 1:
                    root(2 * g + 1)
                if 0 <= x - FIRST_TURN < 8:
                    take_probs(g, x - FIRST_TURN)
                if 0 <= x - FIRST_SCORES < 8:
                    exponentials(g, x - FIRST_SCORES)

            def attention_act(h, first):
                tile0 = h * A_TILES + A_TILE
                for x in range(2 * A_PIECES):
                    if x % 2 == 0:
                        u = x // 2
                        ahead((tile0 + u // PIECES, u % PIECES))
                    if first and x == 0:
                        m_square_sums(M_HEADS - 1)
                    if x == 7:
                        if not first:
                            act.wait_ge(a_vtr, 3 * h)
                        read_out(act, tile0, halves_by_class(a_v))
                    if not first and x not in (15, 23):
                        attention_ops(h - 1, x)
                    if x == 8:
                        act.wait_ge(proj_free, tile_out(tile0))
                        nc.scalar.copy(vcut.rearrange("p e r n -> p r e n"),
                                       by_class(a_v)[:, :, P - EDGE:P + EDGE].rearrange("p r (e n) -> p r e n", e=2)
                                       ).then_inc(a_vcut, 1)
                    if x == 15:
                        if not first:
                            act.wait_ge(a_s, 8 * h)
                        read_out(act, tile0 + 1, halves_by_class(a_q))
                        if not first:
                            attention_ops(h - 1, x)
                    if x == 16:
                        if not first:
                            act.wait_ge(a_t, 16 * h - 2)
                        else:
                            act.wait_ge(m_out, 16 * M_HEADS)
                        act.wait_ge(proj_free, tile_out(tile0 + 1))
                        squares(2 * h, a_q[:])
                    if x == 17:
                        root(2 * h)
                    if x == 18:
                        act.wait_ge(a_vtr, 3 * h + 1)
                        if not first:
                            act.wait_ge(a_pv, 4 * h)
                        nc.scalar.copy(vtok[:, 0:4, :], ps[:, 2, :].rearrange("p (b d) -> p b d", d=P)
                                       ).then_inc(a_va, 1)
                    if x == 23:
                        read_out(act, tile0 + 2, halves_by_class(a_k))

            attention_act(0, True)
            with act.Fori(1, ATT_HEADS) as h:
                attention_act(h, False)

            for x in range(2 * A_PIECES):
                if x % 2 == 0:
                    ahead((Z_TILE + x // 2 // PIECES, x // 2 % PIECES))
                if x % 8 != 7:
                    attention_ops(ATT_HEADS - 1, x)
                else:
                    t = x // 8
                    if t == 0:
                        act.wait_ge(a_vtr, 3 * ATT_HEADS)
                    else:
                        act.wait_ge(a_s, 8 * ATT_HEADS)
                    read_out(act, Z_TILE + t, halves(zs[:, t * SEQ:(t + 1) * SEQ], ACT.Silu))
                    attention_ops(ATT_HEADS - 1, x)
            for t in range(A_TILES, ATT_HEADS):
                for s in range(PIECES):
                    ahead((Z_TILE + t, s))
                if t == A_TILES:
                    act.wait_ge(a_out, 16 * (ATT_HEADS + 1))
                read_out(act, Z_TILE + t, halves(zs[:, t * SEQ:(t + 1) * SEQ], ACT.Silu))

            for kt in range(KT):
                n = kt // 2
                if kt % 2 == 0:
                    act.wait_ge(z_y, n + 1)
                    src = zs[:, n * SEQ:(n + 1) * SEQ]
                else:
                    act.wait_ge(z_in[n % 4], 16 * ((8 + n) // 4 + 1))
                    src = yring[:, n % 4, :]
                if kt == 0:
                    act.wait_ge(w_used, O_PIECE)
                nc.scalar.copy(h_hi[:, kt, :], src).then_inc(o_hi, 1)
            for s in range(PIECES):
                ahead((O_TILE, s))
            with act.Fori(O_TILE + 1, O_TILE + O_TILES - 1) as tile:
                for s in range(PIECES):
                    ahead((tile, s))
            for s in range(PIECES - LEAD):
                ahead((O_TILE + O_TILES - 1, s))

        @block.vector
        def _(dve):
            nc.vector.memset(ones[:], 1.0).then_inc(ones_set, 1)
            dve.wait_ge(consts, 80)
            nc.vector.tensor_scalar(vec[:, 3:4], vec[:, 0:1], -float(P) ** -0.5, None, ALU.mult).then_inc(prep, 1)
            nc.vector.memset(vec[:, 4:5], EPS).then_inc(prep, 1)
            dve.wait_ge(x_rms, 1)
            dve.wait_ge(x_sum, KT)
            nc.vector.reciprocal(xrs[:], xrs[:]).then_inc(x_rs, 1)
            dve.wait_ge(x_rs, 1)

            def low_part(kt):
                dve.wait_ge(h_hid, kt + 1)
                nc.vector.tensor_tensor(h_lo[:, kt, :], hblk[:, kt % 4, :], h_hi[:, kt, :].bitcast(F32), ALU.subtract
                                        ).then_inc(h_lod, 1)
            for kt in range(KT):
                if kt >= 4:
                    dve.wait_ge(h_lod, kt - 3)
                nc.vector.scalar_tensor_tensor(hblk[:, kt % 4, :], x_raw[:, kt, :], ncol[:, kt:kt + 1], xrs[:],
                                               ALU.mult, ALU.mult).then_inc(h_full, 1)
                if kt >= 1:
                    low_part(kt - 1)
                if kt < LEAD:
                    weight_lo(dve, 0, kt)
            low_part(KT - 1)

            def ahead(piece_at):
                tile, s = piece_at
                weight_lo(dve, tile + (s + LEAD) // PIECES, (s + LEAD) % PIECES)

            for s in range(PIECES):
                ahead((0, s))
            dve.wait_ge(h_lod, KT)
            nc.vector.memset(v1[:, :, 256:258], 1.0).then_inc(prep, 1)

            count = [0]

            def g_step(ins):
                ins.then_inc(g_dve, 1)
                count[0] += 1
                dve.wait_ge(g_dve, count[0])

            def gate_rows():
                raw, li, f, m, t, wi = gr
                dve.wait_ge(proj_free, tile_out(0))
                g_step(nc.vector.tensor_copy(li[0:32, :], raw[0:32, :]))
                g_step(nc.vector.tensor_copy(li[32:64, :], raw[32:64, ::-1]))
                g_step(nc.vector.tensor_copy(f[0:32, :], raw[64:96, :]))
                g_step(nc.vector.tensor_copy(f[32:64, :], raw[96:128, ::-1]))
                assert count[0] == GD_SPLIT
                dve.wait_ge(g_act, 3)
                g_step(nc.vector.scalar_tensor_tensor(f[0:64, :], f[0:64, :], 0.0, t[0:64, :], ALU.min, ALU.subtract))
                g_step(nc.vector.tensor_tensor_scan(out=m[0:64, :], data0=f[0:64, :], data1=li[0:64, :], initial=NEG,
                                                    op0=ALU.add, op1=ALU.max))
                g_step(nc.vector.memset(t[0:64, :], 0.0))
                for c in range(TB):
                    cols = slice(c * P, (c + 1) * P)
                    g_step(nc.vector.tensor_tensor_scan(out=raw[0:64, cols], data0=f[0:64, cols], data1=t[0:64, cols],
                                                        initial=0.0, op0=ALU.add, op1=ALU.add))
                g_step(nc.vector.tensor_tensor(f[0:64, :], li[0:64, :], raw[0:64, :], ALU.subtract))
                g_step(nc.vector.tensor_tensor(t[0:64, :], raw[0:64, :], m[0:64, :], ALU.subtract))
                g_step(nc.vector.tensor_scalar(wi[0:64, 0:P], t[0:64, 0:P], NEG, None, ALU.add))
                for c in range(1, TB):
                    g_step(nc.vector.tensor_scalar(wi[0:64, c * P:(c + 1) * P], t[0:64, c * P:(c + 1) * P],
                                                   m[0:64, c * P - 1:c * P], None, ALU.add))
                assert count[0] == GD_INTER
                g_step(nc.vector.tensor_copy(rows[0:32, :], t[0:32, :]))
                g_step(nc.vector.tensor_copy(rows[32:64, :], t[32:64, ::-1]))
                g_step(nc.vector.tensor_copy(li[0:32, :], m[0:32, :]))
                g_step(nc.vector.tensor_copy(li[32:64, :], m[32:64, ::-1]))
                g_step(nc.vector.tensor_copy(m[0:32, :], f[0:32, :]))
                g_step(nc.vector.tensor_copy(m[32:64, :], f[32:64, ::-1]))
                dve.wait_ge(g_act, 4)
                g_step(nc.vector.tensor_copy(rows[64:96, :], wi[0:32, :]))
                g_step(nc.vector.tensor_copy(rows[96:128, :], wi[32:64, ::-1]))
                assert count[0] == GD_ROWS

            def gate_cols():
                dve.wait_ge(g_pe, 1)
                for d in range(2):
                    src = ps[:, 4, :].rearrange("p (c r) -> p c r", r=64)[:, :, 32 * d:32 * d + M_HEADS]
                    g_step(nc.vector.tensor_copy(g_cols[:, :, d, :], src))
                for k in range(4):
                    src = flat(6).rearrange("p (c r) -> p c r", r=P)[:, :, 32 * k:32 * k + M_HEADS]
                    g_step(nc.vector.tensor_copy(a_cols[:, :, k, :], src))

            def m_mask(j, n):
                d, i = n // TB, n % 2
                dve.wait_ge(m_x, 16 * j + n + 1)
                if n >= 2 or not isinstance(j, int) or j > 0:
                    dve.wait_ge(m_kw, 16 * j + n - 1)
                    dve.wait_ge(m_num, 16 * j + n - 1)
                    dve.wait_ge(m_ops, 16 * j + n - 1)
                nc.vector.tensor_tensor(chunkbuf[:, i, 0, :], ps[:, 6, 0:P], tri_m[:, d, :], ALU.add).then_inc(m_t, 1)

            def m_operands(j, n):
                c, d, i = chunk_of(n), n // TB, n % 2
                end = 0 if d else P - 1
                nc.vector.tensor_tensor(chunkbuf[:, i, 2, :], qT[:, c * P:(c + 1) * P], ps[:, 6, P:2 * P], ALU.mult)
                if n >= 2 or not isinstance(j, int) or j > 0:
                    dve.wait_ge(m_c, 16 * j + n - 1)
                nc.vector.tensor_copy(small[:, 8 + i:9 + i], ps[:, 6, P + end:P + end + 1])
                dve.wait_ge(m_w, 16 * j + n + 1)
                nc.vector.tensor_tensor(chunkbuf[:, i, 1, :], ps[:, 6, 2 * P:3 * P], chunkbuf[:, i, 0, :], ALU.mult
                                        ).then_inc(m_ops, 1)

            def m_results(j, n):
                c, d, i = chunk_of(n), n // TB, n % 2
                dve.wait_ge(m_upd, 16 * j + n + 1)
                after = cst[:, (n + 1) % 2, 0:MV]
                if n % TB == 0:
                    nc.vector.tensor_copy(after, ps[:, 5, 0:MV]).then_inc(m_c, 1)
                else:
                    dve.wait_ge(m_c, 16 * j + n)
                    nc.vector.scalar_tensor_tensor(after, cst[:, n % 2, 0:MV], small[:, 8 + i:9 + i], ps[:, 5, 0:MV],
                                                   ALU.mult, ALU.add).then_inc(m_c, 1)
                den = ps[:, 4, 256:257]
                nc.vector.tensor_scalar(small[:, 10:11], den, ec[:, c, d:d + 1], None, ALU.max).then_inc(m_den, 1)
                dve.wait_ge(m_den, 48 * j + 3 * n + 1)
                nc.vector.scalar_tensor_tensor(small[:, 11:12], den, -1.0, small[:, 10:11], ALU.mult, ALU.max
                                               ).then_inc(m_den, 1)
                dve.wait_ge(m_den, 48 * j + 3 * n + 2)
                nc.vector.reciprocal(small[:, 12:13], small[:, 11:12]).then_inc(m_den, 1)
                dve.wait_ge(m_den, 48 * j + 3 * n + 3)
                h_at = hbuf[:, c * 256:(c + 1) * 256]
                if d == 0:
                    nc.vector.tensor_scalar(h_at, ps[:, 4, 0:256], small[:, 12:13], None, ALU.mult).then_inc(m_h, 1)
                else:
                    if n == TB:
                        dve.wait_ge(m_h, 16 * j + n)
                    nc.vector.scalar_tensor_tensor(h_at, ps[:, 4, 0:256], small[:, 12:13], h_at, ALU.mult, ALU.add
                                                   ).then_inc(m_h, 1)

            def m_normalise(j):
                dve.wait_ge(m_rms, j + 1)
                nc.vector.reciprocal(small[:, 32:40], small[:, 24:32]).then_inc(m_rs, 1)
                dve.wait_ge(m_rs, j + 1)
                for c in range(TB):
                    nc.vector.tensor_scalar(hbuf[:, c * 256:(c + 1) * 256], hbuf[:, c * 256:(c + 1) * 256],
                                            small[:, 32 + c:33 + c], None, ALU.mult).then_inc(m_hn, 1)

            def m_outputs(j, e):
                for b in range(2):
                    dve.wait_ge(m_htr, 4 * j + 2 * e + b + 1)
                    at = gate[:, e * SEQ + b * HALF:e * SEQ + (b + 1) * HALF]
                    nc.vector.tensor_tensor(at, ps[:, 2 + b, :], at, ALU.mult).then_inc(m_y, 1)

            def mlstm_dve(j, first):
                tile0 = j * M_TILES + G_TILE
                for u in range(M_PIECES):
                    ahead((tile0 + u // PIECES, u % PIECES))
                    if first and u == 0:
                        gate_rows()
                    if first and u == 4:
                        gate_cols()
                    if not first:
                        if u == 0:
                            m_gates(j - 1, 1)
                            m_normalise(j - 1)
                        if u in (1, 2):
                            m_outputs(j - 1, u - 1)
                    if u in (4, 8):
                        half = u // 4 - 1
                        dve.wait_ge(m_vtr, 4 * j + 2 * half + 2)
                        nc.vector.tensor_copy(v1[:, 4:8, half * P:(half + 1) * P],
                                              ps[:, 3, :].rearrange("p (b d) -> p b d", d=P)).then_inc(m_vd, 1)
                    if u == 28:
                        m_gates(j, 0)
                    if u >= 16:
                        m_results(j, u - 16)
                    if 15 <= u < 31:
                        m_mask(j, u - 15)
                        m_operands(j, u - 15)

            def m_gates(j, e):
                dve.wait_ge(proj_free, tile_out(j * M_TILES + G_TILE + 6 + e))
                at = gate[:, e * SEQ:(e + 1) * SEQ]
                nc.vector.scalar_tensor_tensor(at, vst[:], mw[:, e:e + 1], at, ALU.mult, ALU.mult).then_inc(m_g, 1)

            mw = small[:, 40:42]
            mlstm_dve(0, True)
            with dve.Fori(1, M_HEADS) as j:
                mlstm_dve(j, False)

            def reciprocal_rms(n):
                dve.wait_ge(a_rms, n + 1)
                if not (isinstance(n, int) and n == 0):
                    dve.wait_ge(a_bc, n)
                nc.vector.reciprocal(small[:, 24:32], small[:, 16:24]).then_inc(a_rs, 1)

            def rotate(n, qk, w, part):
                at, tmp = 5 * n, prob[:, 1, :]
                if part == 0:
                    dve.wait_ge(a_bc, n + 1)
                    nc.vector.scalar_tensor_tensor(qk, qk, w, flat(6), ALU.mult, ALU.mult).then_inc(a_rope, 1)
                if part == 1:
                    dve.wait_ge(a_rope, at + 1)
                    nc.vector.memset(small[:, 48:49], 0.0)
                    nc.vector.stream_shuffle(tmp[0:ROT, :], qk[0:ROT, :], mask=[(r + ROT // 2) % ROT for r in range(ROT)]
                                             ).then_inc(a_rope, 1)
                    dve.wait_ge(a_rope, at + 2)
                    nc.vector.tensor_tensor(tmp[0:ROT, :], tmp[0:ROT, :], sin[0:ROT, :], ALU.mult).then_inc(a_rope, 1)
                if part == 2:
                    nc.vector.tensor_tensor(qk[0:ROT, :], qk[0:ROT, :], cos[0:ROT, :], ALU.mult).then_inc(a_rope, 1)
                    dve.wait_ge(a_rope, at + 4)
                    nc.vector.tensor_tensor(qk[0:ROT, :], qk[0:ROT, :], tmp[0:ROT, :], ALU.add).then_inc(a_rope, 1)

            def masked(g, i):
                h, c = divmod(i, CLASSES)
                dve.wait_ge(a_s, 8 * g + i + 1)
                if i >= 2:
                    dve.wait_ge(a_t, 16 * g + 2 * i - 2)
                nc.vector.memset(small[:, 48:49], 0.0)
                at = P * (CLASSES - 1 - c)
                nc.vector.tensor_tensor_reduce(prob[:, i % 2, 0:4 * P], psS[:, 0:4 * P], mask_a[:, at:at + 4 * P], 1.0,
                                               -3 * NEG, ALU.add, ALU.min, small[:, 6 + i % 2:7 + i % 2]
                                               ).then_inc(a_mh, 1)
                dve.wait_ge(a_mh, 8 * g + i + 1)
                nc.vector.memset(small[:, 48:49], 0.0)
                nc.vector.tensor_tensor_reduce(prob[:, i % 2, 4 * P:KEYS], psS[:, 4 * P:KEYS], mask_b[:, i, :], 1.0,
                                               small[:, 6 + i % 2:7 + i % 2], ALU.add, ALU.min,
                                               small[:, i % 2:i % 2 + 1]).then_inc(a_m, 1)

            def normalised(g, i):
                dve.wait_ge(a_e, 8 * g + i + 1)
                nc.vector.reciprocal(small[:, 4 + i % 2:5 + i % 2], small[:, 2 + i % 2:3 + i % 2]).then_inc(a_r, 1)
                dve.wait_ge(a_r, 8 * g + i + 1)
                nc.vector.tensor_scalar(prob[:, i % 2, 0:KEYS], prob[:, i % 2, 0:KEYS],
                                        small[:, 4 + i % 2:5 + i % 2], None, ALU.mult).then_inc(a_p, 1)

            def attention_ops(g, x):
                if x == 1:
                    reciprocal_rms(2 * g + 1)
                if x in (2, 3, 4):
                    rotate(2 * g + 1, a_k, vec[:, 1:2], x - 2)
                if 0 <= x - FIRST_SCORES - 1 < 8:
                    normalised(g, x - FIRST_SCORES - 1)
                i = x - FIRST_TURN
                if 0 <= i < 8:
                    dve.wait_ge(a_t, 16 * g + 2 * i + 2)
                    if i == 0:
                        dve.wait_ge(a_rope, 10 * g + 10)
                    if i % 2 == 0 and i > 0:
                        dve.wait_ge(a_pv, 4 * g + i // 2)
                    nc.vector.tensor_copy(pT[:, 4:6, (i % 2) * P:(i % 2 + 1) * P],
                                          ps[:, 3, 0:256].rearrange("p (b q) -> p b q", q=P)).then_inc(a_td, 1)
                if 0 <= x - FIRST_SCORES < 8:
                    masked(g, x - FIRST_SCORES)
                if i >= 2 and i % 2 == 0 and i <= 8:
                    j = i // 2 - 1
                    h, c = j // 2, 2 * (j % 2)
                    dve.wait_ge(a_pv, 4 * g + j + 1)
                    if j == 0:
                        dve.wait_ge(a_out, 16 * (g + 1))
                    nc.vector.tensor_copy(
                        ystage.rearrange("p (n r) -> p r n", r=CLASSES)[:, c:c + 2, h * P:(h + 1) * P],
                        ps[:, 6 + j % 2, 0:256].rearrange("p (r n) -> p r n", n=P)).then_inc(a_y, 1)

            def attention_dve(h, first):
                tile0 = h * A_TILES + A_TILE
                for x in range(2 * A_PIECES):
                    if x % 2 == 0:
                        u = x // 2
                        ahead((tile0 + u // PIECES, u % PIECES))
                    if first and x == 0:
                        m_gates(M_HEADS - 1, 1)
                        m_normalise(M_HEADS - 1)
                    if first and x in (3, 5):
                        m_outputs(M_HEADS - 1, (x - 3) // 2)
                    if not first:
                        attention_ops(h - 1, x)
                    if x == 17:
                        reciprocal_rms(2 * h)
                    if x == 18:
                        dve.wait_ge(a_vtr, 3 * h + 2)
                        nc.vector.tensor_copy(vtok[:, 4:8, :], ps[:, 3, :].rearrange("p (b d) -> p b d", d=P)
                                              ).then_inc(a_vd, 1)
                        dve.wait_ge(a_vtr, 3 * h + 3)
                        nc.vector.tensor_copy(vedge[0:CLASSES * EDGE],
                                              ps[0:CLASSES * EDGE, 4, 0:256].rearrange("p (h d) -> p h d", d=P)
                                              ).then_inc(a_ve, 1)
                    if x in (19, 20, 21):
                        if x == 20:
                            dve.wait_ge(a_cs, 32 * h + 32)
                            if not first:
                                dve.wait_ge(a_t, 16 * h)
                        rotate(2 * h, a_q, vec[:, 3:4], x - 19)

            attention_dve(0, True)
            with dve.Fori(1, ATT_HEADS) as h:
                attention_dve(h, False)

            def gated(t):
                dve.wait_ge(proj_free, tile_out(Z_TILE + t))
                dve.wait_ge(z_in[t % 4], 16 * (t // 4 + 1))
                at = zs[:, t * SEQ:(t + 1) * SEQ]
                nc.vector.tensor_tensor(at, at, yring[:, t % 4, :], ALU.mult).then_inc(z_y, 1)

            for x in range(2 * A_PIECES):
                if x % 2 == 0:
                    ahead((Z_TILE + x // 2 // PIECES, x // 2 % PIECES))
                attention_ops(ATT_HEADS - 1, x)
            for t in range(A_TILES, ATT_HEADS):
                for s in range(PIECES):
                    ahead((Z_TILE + t, s))
                    if t == A_TILES and s >= 1:
                        gated(s - 1)
                    if t > A_TILES and s == 1:
                        gated(t - 1)
            gated(ATT_HEADS - 1)

            for kt in range(KT):
                n = kt // 2
                src = zs[:, n * SEQ:(n + 1) * SEQ] if kt % 2 == 0 else yring[:, n % 4, :]
                dve.wait_ge(o_hi, kt + 1)
                nc.vector.tensor_tensor(h_lo[:, kt, :], src, h_hi[:, kt, :].bitcast(F32), ALU.subtract
                                        ).then_inc(o_lo, 1)

            def output(tile, i, n2, first):
                dve.wait_ge(o_x[i], 16 * (n2 + 1))
                if not first:
                    dve.wait_ge(o_out[i], 16 * n2)
                read_out(dve, tile, lambda k: nc.vector.tensor_tensor(
                    oblk[:, i, k * HALF:(k + 1) * HALF], psP[:, k, :], xres[:, i, k * HALF:(k + 1) * HALF], ALU.add))

            for i in range(2):
                for s in range(PIECES):
                    ahead((O_TILE + i, s))
                if i == 0:
                    dve.wait_ge(o_lo, KT)
                output(O_TILE + i, i, 0, True)
            with dve.Fori(1, O_TILES // 2 - 1) as n2:
                for i in range(2):
                    for s in range(PIECES):
                        ahead((n2 * 2 + O_TILE + i, s))
                    output(n2 * 2 + O_TILE + i, i, n2, False)
            last = O_TILES // 2 - 1
            for i in range(2):
                for s in range(PIECES if i == 0 else PIECES - LEAD):
                    ahead((O_TILE + 2 * last + i, s))
                output(O_TILE + 2 * last + i, i, last, False)

        @block.gpsimd
        def _(pool):
            pool.wait_ge(consts, 80)

            nc.gpsimd.memset(small[:, 50:51], 0.0).then_inc(p_held, 1)

            def held(k):
                pool.wait_ge(p_held, k + 1)
                nc.gpsimd.tensor_tensor(small[:, 51:52], small[:, 50:51], small[:, 50:51], ALU.add
                                        ).then_inc(p_held, 1)

            def select(j, first):
                if first:
                    pool.wait_ge(g_dve, GD_COLS)
                    pool.wait_ge(g_act, 6)
                    pool.wait_ge(prep, 3)
                else:
                    pool.wait_ge(m_h, 16 * j)
                    pool.wait_ge(m_g, 2 * j)
                at = 3 * j
                nc.gpsimd.tensor_copy(ac.rearrange("p c k d -> p c (k d)"),
                                      a_cols[:, :, :, bass.ds(j, 1)].rearrange("p c k h -> p c (k h)")
                                      ).then_inc(m_pick, 1)
                pool.wait_ge(m_pick, at + 1)
                nc.gpsimd.tensor_copy(gc[:], g_cols[:, :, :, bass.ds(j, 1)].rearrange("p c d h -> p c (d h)")
                                      ).then_inc(m_pick, 1)
                pool.wait_ge(m_pick, at + 2)
                nc.gpsimd.tensor_copy(small[:, 40:42], mcol[:, bass.ds(2 * j, 2)]).then_inc(m_pick, 1)
                pool.wait_ge(m_pick, at + 3)
                nc.gpsimd.tensor_copy(ec[:], e_cols[:, :, :, bass.ds(j, 1)].rearrange("p c d h -> p c (d h)")
                                      ).then_inc(m_sel, 1)

            def store_mlstm(j):
                pool.wait_ge(m_y, 4 * j + 4)
                if not isinstance(j, int):
                    held(j)
                pool.dma_start(y_dram[bass.ds(2 * j + ATT_HEADS, 2)].rearrange("e p t -> p e t"),
                               gate.rearrange("p (e t) -> p e t", e=2)).then_inc(m_out, 16)

            select(0, True)
            with pool.Fori(1, M_HEADS) as j:
                select(j, False)
                store_mlstm(j - 1)
            store_mlstm(M_HEADS - 1)
            pool.wait_ge(m_h, 16 * M_HEADS)
            pool.wait_ge(m_out, 16 * M_HEADS)
            pool.dma_start(view(5120, MASK_A + 8 * MASK_B), att_mask).then_inc(a_out, 16)

            def tables():
                pool.dma_start(cos[0:ROT, :], rope[0]).then_inc(a_cs, 16)
                pool.dma_start(sin[0:ROT, :], rope[1]).then_inc(a_cs, 16)

            def store_attention(h):
                pool.dma_start(y_dram[bass.ds(h, 1)].rearrange("e p t -> p (e t)"), ystage).then_inc(a_out, 16)

            tables()
            with pool.Fori(1, ATT_HEADS) as h:
                pool.wait_ge(a_pv, 4 * h)
                held(2 * h + M_HEADS - 3)
                tables()
                pool.wait_ge(a_y, 4 * h)
                held(2 * h + M_HEADS - 2)
                store_attention(h - 1)
            pool.wait_ge(a_y, 4 * ATT_HEADS)
            store_attention(ATT_HEADS - 1)

            pool.wait_ge(a_pv, 4 * ATT_HEADS)
            for n in range(ATT_HEADS + 2 * M_HEADS):
                if n == ATT_HEADS - 1:
                    pool.wait_ge(a_out, 16 * (ATT_HEADS + 1))
                if n == 0:
                    pool.wait_ge(a_out, 16 * ATT_HEADS)
                if n - 4 >= ATT_HEADS:
                    pool.wait_ge(o_lo, 2 * (n - 4 - ATT_HEADS) + 2)
                elif n >= 4:
                    pool.wait_ge(z_y, n - 3)
                pool.dma_start(yring[:, n % 4, :], y_dram[n]).then_inc(z_in[n % 4], 16)
            pool.wait_ge(o_lo, KT)
            for i in range(2):
                pool.dma_start(xres[:, i, :], xT[i]).then_inc(o_x[i], 16)
            with pool.Fori(0, O_TILES // 2 - 1) as n2:
                for i in range(2):
                    pool.wait_ge(proj_free, tile_out(n2 * 2 + O_TILE + i))
                    held(2 * n2 + M_HEADS - 1 + 2 * (ATT_HEADS - 1) + i)
                    pool.dma_start(outT[bass.ds(2 * n2 + i, 1)].rearrange("a p t -> p (a t)"), oblk[:, i, :]
                                   ).then_inc(o_out[i], 16)
                    pool.dma_start(xres[:, i, :], xT[bass.ds(2 * n2 + 2 + i, 1)].rearrange("a p t -> p (a t)")
                                   ).then_inc(o_x[i], 16)
            for i in range(2):
                pool.wait_ge(proj_free, tile_out(O_TILE + O_TILES - 2 + i))
                pool.dma_start(outT[O_TILES - 2 + i], oblk[:, i, :]).then_inc(o_out[i], 16)
            for i in range(2):
                pool.wait_ge(o_out[i], 16 * (O_TILES // 2))


GD_SPLIT = 4
GD_INTER = GD_SPLIT + 3 + TB + 2 + TB
GD_ROWS = GD_INTER + 8
GD_COLS = GD_ROWS + 6


def shape_constants():
    pos = np.arange(SEQ, dtype=np.float32)
    inv = (500000.0 ** (-np.arange(0, ROT, 2, dtype=np.float32) / ROT)).astype(np.float32)
    ang = (pos[:, None] * inv[None, :]).astype(np.float32).T
    c, s = np.cos(ang), np.sin(ang)
    rope = np.stack([np.concatenate([c, c]), np.concatenate([-s, s])]).astype(np.float32)
    rope = np.ascontiguousarray(rope.reshape(2, ROT, SEQ // CLASSES, CLASSES).transpose(0, 1, 3, 2)).reshape(2, ROT, SEQ)

    def entry(rel):
        n = np.zeros(rel.shape)
        for window, dil in ((128, 1), (512, 4), (2048, 16)):
            n += (rel % dil == 0) & (np.abs(rel) // dil <= window // (2 * dil))
        return np.where(n > 0, -np.log(np.maximum(n, 1)), -NEG)

    query, place = np.arange(P)[:, None], np.arange(P)[None, :]
    tables = [entry(4 * (place - query) + diff) for diff in range(1 - CLASSES, CLASSES)]
    for half in range(2):
        for own in range(CLASSES):
            for c in range(CLASSES):
                e = place[:, :EDGE] + (P if half == 0 else -EDGE)
                edge = entry(4 * (e - query) + c - own)
                tables.append(np.full_like(edge, -NEG) if c == own else edge)
            tables.append(entry(4 * (place + (P if half == 0 else -P) - query)))
    table = np.concatenate(tables, axis=1).astype(np.float32)
    s_, t_ = np.arange(P)[:, None], np.arange(P)[None, :]
    tri = np.stack([np.where(s_ <= t_, 0.0, NEG), np.where(s_ >= t_, 0.0, NEG)], axis=1).astype(np.float32)
    return rope, table, np.eye(P, dtype=np.float32), tri


def weight_pieces(w):
    n = w.shape[1] // P
    return w.reshape(PIECES, KP, P, n, P).transpose(3, 0, 2, 1, 4).reshape(n * PIECES, P, KP * P)


def kernel(x, norm_w, w_in, b_gates, q_norm_w, k_norm_w, m_norm_w, w_out):
    import numpy as _np
    import concourse.bacc as _bacc
    from concourse import mybir as _mybir
    from concourse.bass_utils import run_bass_kernel_spmd as _run

    x, norm_w, w_in, b_gates, q_norm_w, k_norm_w, m_norm_w, w_out = (
        _np.asarray(a) for a in (x, norm_w, w_in, b_gates, q_norm_w, k_norm_w, m_norm_w, w_out))
    w = w_in[0]
    qa, ka, va, za, qm, km, vm, om, zm, g = _np.split(
        w, _np.cumsum([1024, 1024, 1024, 1024, 512, 512, 1024, 1024, 1024]).tolist(), axis=1)
    gates = _np.zeros((D_MODEL, P), w.dtype)
    bias = _np.zeros(P, w.dtype)
    for at, k in ((0, 0), (64, 1), (32, 2), (96, 3)):
        gates[:, at:at + M_HEADS] = g[:, k * M_HEADS:(k + 1) * M_HEADS]
        bias[at:at + M_HEADS] = b_gates[0, k * M_HEADS:(k + 1) * M_HEADS]
    cols = [gates]
    for j in range(M_HEADS):
        cols += [vm[:, 256 * j:256 * (j + 1)], km[:, P * j:P * (j + 1)], qm[:, P * j:P * (j + 1)],
                 om[:, 256 * j:256 * (j + 1)], zm[:, 256 * j:256 * (j + 1)]]
    for h in range(ATT_HEADS):
        cols += [a[:, P * h:P * (h + 1)] for a in (va, qa, ka)]
    cols.append(za)
    wo = w_out[0].reshape(2, ATT_HEADS, P, D_MODEL).transpose(1, 0, 2, 3).reshape(D_MODEL, D_MODEL)
    w_all = _np.ascontiguousarray(weight_pieces(_np.concatenate(cols + [wo], axis=1)))
    rope, table, eye, tri = shape_constants()
    vecs = _np.zeros((P, 8), w.dtype)
    vecs[:, 0], vecs[:, 1], vecs[:, 2] = q_norm_w[0], k_norm_w[0], bias
    arrays = {
        "xT_dram": _np.ascontiguousarray(x[0].T).reshape(KT, P, SEQ),
        "w_all_dram": w_all,
        "vecs_dram": vecs,
        "norm_cols_dram": _np.ascontiguousarray(norm_w[0].reshape(KT, P).T),
        "m_cols_dram": _np.ascontiguousarray(m_norm_w[0].reshape(8, P).T),
        "att_mask_dram": table,
        "rope_dram": rope,
        "eye_dram": eye,
        "tri_dram": tri,
    }
    nc = _bacc.Bacc("TRN2", target_bir_lowering=False, num_devices=1)
    args = [nc.dram_tensor(n, a.shape, _mybir.dt.float32, kind="ExternalInput").ap() for n, a in arrays.items()]
    y_dram = nc.dram_tensor("y_dram", (KT, P, SEQ), _mybir.dt.float32, kind="Internal").ap()
    outT = nc.dram_tensor("outT_dram", (O_TILES, P, SEQ), _mybir.dt.float32, kind="ExternalOutput").ap()
    build_program(nc, *args, y_dram, outT)
    r = _run(nc, [arrays], core_ids=[0])
    return _np.ascontiguousarray(r.results[0]["outT_dram"].reshape(D_MODEL, SEQ).T).reshape(1, SEQ, D_MODEL)
```

```python
from contextlib import ExitStack

import numpy as np

import concourse.bass as bass
from concourse import mybir

F32 = mybir.dt.float32
F32R = mybir.dt.float32r
ALU = mybir.AluOpType
ACT = mybir.ActivationFunctionType

P = 128
D_MODEL = 2048
SEQ = 1024
KT = D_MODEL // P
HALF = 512
TB = SEQ // P
PIECES = 4
KP = KT // PIECES
LEAD = 3
GATE_STEPS = (0, 2, 3, 4, 5)
AHEAD_OF_GATES = (3, 11, 14)

ATT_HEADS = 8
ROT = 32
M_HEADS = 4
A_TILES = 3
M_TILES = 8
A_PIECES = A_TILES * PIECES
M_PIECES = M_TILES * PIECES
G_PIECE = PIECES
A_PIECE = G_PIECE + M_HEADS * M_PIECES
Z_PIECE = A_PIECE + ATT_HEADS * A_PIECES
O_PIECE = Z_PIECE + ATT_HEADS * PIECES
O_TILES = D_MODEL // P
N_PIECE = O_PIECE + O_TILES * PIECES
G_TILE, A_TILE, Z_TILE, O_TILE = (n // PIECES for n in (G_PIECE, A_PIECE, Z_PIECE, O_PIECE))

EPS = 1e-6
SQ_RING = 8
NEG = -1e30
V1 = 258
MV = 257
STEPS = 2 * TB
CLASSES = 4
EDGE = 16
KEYS = 4 * P + CLASSES * EDGE + P
MASK_A = (2 * CLASSES - 1) * P
MASK_B = KEYS - 4 * P
FIRST_SCORES, FIRST_TURN = 7, 9


def chunk_of(n):
    return n if n < TB else STEPS - 1 - n


def build_program(nc, xT, w_all, vecs, norm_cols, m_cols, att_mask, rope, eye, tri, y_dram, outT):
    with ExitStack() as ctx:
        def sb(name, shape, dt=F32):
            return ctx.enter_context(nc.sbuf_tensor(name, shape, dt))

        def sem(name):
            return ctx.enter_context(nc.semaphore(name))

        h_hi = sb("h_hi", [P, KT, SEQ], F32R)
        h_lo = sb("h_lo", [P, KT, SEQ], F32R)
        h_lo_end = nc.sbuf_base
        w_raw = sb("w_raw", [P, PIECES, KP * P])
        w_hi = sb("w_hi", [P, PIECES, KP * P], F32R)
        w_lo = sb("w_lo", [P, PIECES, KP * P], F32R)
        ident = sb("ident", [P, P])
        ones = sb("ones", [P, P])
        vec = sb("vec", [P, 8])
        ncol = sb("ncol", [P, KT])
        mcol = sb("mcol", [P, 8])
        tri_m = sb("tri_m", [P, 2, P])
        small = sb("small", [P, 64])
        xrs = sb("xrs", [P, SEQ])
        g_cols = sb("g_cols", [P, TB, 2, M_HEADS])
        e_cols = sb("e_cols", [P, TB, 2, M_HEADS])
        a_cols = sb("a_cols", [P, TB, 4, M_HEADS])
        A_FL = 12344
        arena = sb("arena", [P, A_FL])

        def view(at, n):
            return arena[:, at:at + n]

        qT, kT = view(0, 1024), view(1024, 1024)
        hbuf = view(2048, 2048)
        gate = view(4096, 2048)
        vst = view(6144, 1024)
        v1 = view(7168, TB * V1).rearrange("p (c e) -> p c e", e=V1)
        rows = view(9232, 1024)
        chunkbuf = view(10256, 2 * 4 * P).rearrange("p (i k t) -> p i k t", i=2, k=4)
        cst = view(11280, 2 * V1).rearrange("p (i e) -> p i e", e=V1)
        ac = view(11796, 4 * TB).rearrange("p (c k d) -> p c k d", k=2, d=2)
        gc = view(12308, 2 * TB).rearrange("p (c d) -> p c d", d=2)
        ec = view(12324, 2 * TB).rearrange("p (c d) -> p c d", d=2)
        a_v = view(0, 1024)
        a_q, a_k = view(1024, 1024), view(2048, 1024)
        prob = view(3072, 2048).rearrange("p (i k) -> p i k", i=2)
        mask_a = view(5120, MASK_A)
        mask_b = view(5120 + MASK_A, 8 * MASK_B).rearrange("p (i k) -> p i k", i=8)
        ystage = view(7552, 1024)
        vtok = view(8576, 1024).rearrange("p (b d) -> p b d", d=P)
        vedge = view(9600, 256).rearrange("p (h d) -> p h d", d=P)
        pT = view(9856, 6 * 256).rearrange("p (b q) -> p b q", b=6)
        cos, sin = view(9856, 1024), view(10880, 1024)
        vcut = view(11904, 2 * CLASSES * EDGE).rearrange("p (e r n) -> p e r n", e=2, r=CLASSES)
        zs = view(0, 8 * SEQ)
        yring = view(8192, 4 * SEQ).rearrange("p (i t) -> p i t", i=4)
        gr = [view(2048 + 1024 * i, 1024) for i in range(4)] + [qT, kT]
        x_raw = nc.alloc_sbuf_tensor_at("x_raw", [P, KT, SEQ], F32, offset=h_lo_end - KT * SEQ * 4)
        xsq = view(2048, SQ_RING * SEQ).rearrange("p (i t) -> p i t", i=SQ_RING)
        oblk = view(0, 2 * SEQ).rearrange("p (i t) -> p i t", i=2)
        xres = view(2048, 2 * SEQ).rearrange("p (i t) -> p i t", i=2)

        ps = ctx.enter_context(nc.psum_tensor("ps", [P, 8, HALF], F32))
        psP = ps[:, 0:2, :]
        psS = ps[:, 4:6, :].rearrange("p b k -> p (b k)")

        def by_class(row):
            return row.rearrange("p (r n) -> p r n", r=CLASSES)

        def flat(b):
            return ps[:, b:b + 2, :].rearrange("p b k -> p (b k)")

        w_landed = [sem(f"w_landed{i}") for i in range(PIECES)]
        w_hi_done = sem("w_hi_done")
        w_lo_done = sem("w_lo_done")
        w_used = sem("w_used")
        half_done = sem("half_done")
        proj_free = sem("proj_free")
        consts = sem("consts")
        ones_set = sem("ones_set")
        x_in = [sem(f"x_in{i}") for i in range(KT)]
        x_sq = sem("x_sq")
        x_pair = sem("x_pair")
        x_sum = sem("x_sum")
        x_rms = sem("x_rms")
        x_rs = sem("x_rs")
        x_bc = sem("x_bc")
        x_norm = sem("x_norm")
        h_hid = sem("h_hid")
        h_hiv = sem("h_hiv")
        h_lod = sem("h_lod")
        prep = sem("prep")
        g_act = sem("g_act")
        g_dve = sem("g_dve")
        g_pe = sem("g_pe")
        m_sel = sem("m_sel")
        m_pick = sem("m_pick")
        m_vtr = sem("m_vtr")
        m_va = sem("m_va")
        m_vd = sem("m_vd")
        m_x = sem("m_x")
        m_t = sem("m_t")
        m_w = sem("m_w")
        m_ops = sem("m_ops")
        m_kw = sem("m_kw")
        m_num = sem("m_num")
        m_upd = sem("m_upd")
        m_c = sem("m_c")
        m_den = sem("m_den")
        m_h = sem("m_h")
        m_act = sem("m_act")
        m_g = sem("m_g")
        m_ss = sem("m_ss")
        m_rms = sem("m_rms")
        m_rs = sem("m_rs")
        m_hn = sem("m_hn")
        m_htr = sem("m_htr")
        m_y = sem("m_y")
        m_out = sem("m_out")
        p_held = sem("p_held")
        a_sq = sem("a_sq")
        a_ssum = sem("a_ssum")
        a_rms = sem("a_rms")
        a_rs = sem("a_rs")
        a_bc = sem("a_bc")
        a_rope = sem("a_rope")
        a_cs = sem("a_cs")
        a_s = sem("a_s")
        a_mh = sem("a_mh")
        a_m = sem("a_m")
        a_e = sem("a_e")
        a_r = sem("a_r")
        a_p = sem("a_p")
        a_t = sem("a_t")
        a_ta = sem("a_ta")
        a_td = sem("a_td")
        a_pv = sem("a_pv")
        a_y = sem("a_y")
        a_vcut = sem("a_vcut")
        a_vtr = sem("a_vtr")
        a_va = sem("a_va")
        a_vd = sem("a_vd")
        a_out = sem("a_out")
        z_in = [sem(f"z_in{i}") for i in range(4)]
        z_act = sem("z_act")
        z_y = sem("z_y")
        o_hi = sem("o_hi")
        o_lo = sem("o_lo")
        o_x = [sem(f"o_x{i}") for i in range(2)]
        o_out = [sem(f"o_out{i}") for i in range(2)]

        block = ctx.enter_context(nc.Block())

        @block.sync
        def _(sp):
            sp.dma_start(vec[:], vecs).then_inc(consts, 16)
            sp.dma_start(ncol[:], norm_cols).then_inc(consts, 16)
            sp.dma_start(mcol[:], m_cols).then_inc(consts, 16)
            sp.dma_start(ident[:], eye).then_inc(consts, 16)
            sp.dma_start(tri_m[:], tri).then_inc(consts, 16)
            for kt in range(KT):
                sp.dma_start(x_raw[:, kt, :], xT[kt]).then_inc(x_in[kt], 16)
                if kt < PIECES:
                    sp.dma_start(w_raw[:, kt, :], w_all[kt]).then_inc(w_landed[kt], 16)
            with sp.Fori(1, N_PIECE // PIECES) as tile:
                for s in range(PIECES):
                    sp.wait_ge(w_lo_done, (tile - 1) * PIECES + s + 1)
                    sp.dma_start(w_raw[:, s, :], w_all[bass.ds(tile * PIECES + s, 1)].rearrange("a p n -> p (a n)")
                                 ).then_inc(w_landed[s], 16)

        def weight_hi(act, tile, s):
            act.wait_ge(w_landed[s], (tile + 1) * 16)
            if not (isinstance(tile, int) and tile == 0):
                act.wait_ge(w_used, (tile - 1) * PIECES + s + 1)
            nc.scalar.copy(w_hi[:, s, :], w_raw[:, s, :]).then_inc(w_hi_done, 1)

        def weight_lo(dve, tile, s):
            dve.wait_ge(w_hi_done, tile * PIECES + s + 1)
            nc.vector.tensor_tensor(w_lo[:, s, :], w_raw[:, s, :], w_hi[:, s, :].bitcast(F32), ALU.subtract
                                    ).then_inc(w_lo_done, 1)

        def piece(pe, tile, s, between=None, per_block=None):
            start = isinstance(tile, int) and tile == 0
            pe.wait_ge(w_lo_done, tile * PIECES + s + 1)
            for i in range(2):
                if s == 0 and not start:
                    pe.wait_ge(proj_free, 2 * tile - 1 + i)
                for j in range(KP):
                    kt = s * KP + j
                    if per_block is not None and i == 0:
                        per_block(kt)
                    hi = w_hi[:, s, j * P:(j + 1) * P]
                    lo = w_lo[:, s, j * P:(j + 1) * P]
                    cols = slice(i * HALF, (i + 1) * HALF)
                    nc.tensor.matmul(psP[:, i, :], hi, h_hi[:, kt, cols], start=kt == 0, stop=False)
                    nc.tensor.matmul(psP[:, i, :], hi, h_lo[:, kt, cols], start=False, stop=False)
                    mm = nc.tensor.matmul(psP[:, i, :], lo, h_hi[:, kt, cols], start=False, stop=kt == KT - 1)
                if i == 0 and s == PIECES - 1:
                    mm.then_inc(half_done, 1)
                if i == 1:
                    mm.then_inc(w_used, 1)
                if between is not None:
                    between(i)

        def read_out(eng, tile, emit):
            eng.wait_ge(half_done, tile + 1)
            emit(0).then_inc(proj_free, 1)
            eng.wait_ge(w_used, (tile + 1) * PIECES)
            emit(1).then_inc(proj_free, 1)

        def tile_out(tile):
            return 2 * tile + 2

        @block.tensor
        def _(pe):
            pe.wait_ge(ones_set, 1)
            pe.wait_ge(consts, 80)
            def transposes(src, bank, n, done):
                for b in range(n):
                    t = nc.tensor.transpose(ps[:, bank + b // 4, (b % 4) * P:(b % 4 + 1) * P], src(b), ident[:])
                    if b % 4 == 3:
                        t.then_inc(done, 1)

            def on_all_partitions(out, column):
                return nc.tensor.transpose(out, column.to_broadcast([P, P]), ident[:])

            def block_made(kt):
                pe.wait_ge(h_lod, kt + 1)

            def sum_squares(k):
                pe.wait_ge(x_pair, k + 1)
                for b in range(TB):
                    mm = nc.tensor.matmul(ps[:, 5, b:b + 1], xsq[:, (2 * k + 1) % SQ_RING, b * P:(b + 1) * P],
                                          ones[:, 0:1], start=k == 0 and b == 0, stop=k == KT // 2 - 1,
                                          skip_group_check=True)
                mm.then_inc(x_sum, 1)

            def behind(s, i):
                if 2 * s + i >= 1:
                    sum_squares(2 * s + i - 1)
            for s in range(PIECES):
                piece(pe, 0, s, between=lambda i: behind(s, i), per_block=block_made)
            sum_squares(KT // 2 - 1)

            def spread_x():
                pe.wait_ge(x_rs, 1)
                for b in range(TB):
                    t = on_all_partitions(flat(6)[:, b * P:(b + 1) * P], small[:, 24 + b:25 + b])
                t.then_inc(x_bc, 1)

            def gate_columns():
                pe.wait_ge(g_dve, GD_ROWS)
                for b in range(2 * TB):
                    src = (gr[3] if b < TB else gr[1])[0:64, (b % TB) * P:(b % TB + 1) * P]
                    nc.tensor.transpose(ps[:, 4 + b // TB, (b % TB) * 64:(b % TB + 1) * 64], src, ident[0:64, 0:64])
                for b in range(TB):
                    t = nc.tensor.transpose(flat(6)[:, b * P:(b + 1) * P], rows[:, b * P:(b + 1) * P], ident[:])
                t.then_inc(g_pe, 1)

            def step_inputs(j, n):
                c, d = chunk_of(n), n // TB
                cols = slice(c * P, (c + 1) * P)
                if n == 0:
                    pe.wait_ge(m_sel, j + 1)
                    pe.wait_ge(proj_free, tile_out(j * M_TILES + G_TILE + 3))
                if n > 0 or not isinstance(j, int) or j > 0:
                    pe.wait_ge(m_ops, 16 * j + n)
                    pe.wait_ge(m_kw, 16 * j + n)
                on_all_partitions(ps[:, 6, 0:P], ac[:, c, 0, d:d + 1])
                on_all_partitions(ps[:, 6, P:2 * P], ac[:, c, 1, d:d + 1])
                nc.tensor.matmul(ps[:, 6, 2 * P:3 * P], kT[:, cols], qT[:, cols], start=True, stop=True)
                nc.tensor.transpose(ps[:, 7, 0:P], kT[:, cols], ident[:]).then_inc(m_x, 1)

            def step_products(j, n):
                c, i = chunk_of(n), n % 2
                first = n % TB == 0
                pe.wait_ge(m_ops, 16 * j + n + 1)
                if n == 0:
                    pe.wait_ge(m_va, 2 * j + 2)
                    pe.wait_ge(m_vd, 2 * j + 2)
                if n > 0 or not isinstance(j, int) or j > 0:
                    pe.wait_ge(m_h, 16 * j + n)
                mm = nc.tensor.matmul(ps[:, 4, 0:MV], chunkbuf[:, i, 1, :], v1[:, c, 0:MV], start=True, stop=first)
                if not first:
                    pe.wait_ge(m_c, 16 * j + n)
                    mm = nc.tensor.matmul(ps[:, 4, 0:MV], chunkbuf[:, i, 2, :], cst[:, n % 2, 0:MV],
                                          start=False, stop=True)
                mm.then_inc(m_num, 1)
                pe.wait_ge(m_kw, 16 * j + n + 1)
                if first and (n > 0 or not isinstance(j, int) or j > 0):
                    pe.wait_ge(m_c, 16 * j + n)
                nc.tensor.matmul(ps[:, 5, 0:MV], chunkbuf[:, i, 3, :], v1[:, c, 0:MV], start=True, stop=True
                                 ).then_inc(m_upd, 1)

            def m_value_transposes(j, half):
                pe.wait_ge(proj_free, tile_out(j * M_TILES + G_TILE + half))
                if half == 1:
                    pe.wait_ge(m_va, 2 * j + 1)
                    pe.wait_ge(m_vd, 2 * j + 1)
                elif not (isinstance(j, int) and j == 0):
                    pe.wait_ge(m_y, 4 * j)
                transposes(lambda b: vst[:, b * P:(b + 1) * P], 2, TB, m_vtr)

            def m_output_transposes(j, e):
                pe.wait_ge(m_hn, 8 * j + 8)
                if e == 1:
                    pe.wait_ge(m_y, 4 * j + 2)
                transposes(lambda b: hbuf[:, b * 256 + e * P:b * 256 + (e + 1) * P], 2, TB, m_htr)

            def mlstm_pe(j, first):
                for u in range(M_PIECES):
                    piece(pe, j * M_TILES + G_TILE + u // PIECES, u % PIECES)
                    if first and u == 0:
                        spread_x()
                    if first and u == GATE_STEPS[-1] + 1:
                        gate_columns()
                    if not first and u in (1, 2):
                        m_output_transposes(j - 1, u - 1)
                    if u in (4, 8):
                        m_value_transposes(j, u // 4 - 1)
                    if u >= 16:
                        step_products(j, u - 16)
                    if 15 <= u < 31:
                        step_inputs(j, u - 15)

            mlstm_pe(0, True)
            with pe.Fori(1, M_HEADS) as j:
                mlstm_pe(j, False)

            def square_sums(n):
                pe.wait_ge(a_sq, n + 1)
                for b in range(TB):
                    mm = nc.tensor.matmul(ps[:, 5, b:b + 1], prob[:, 0, b * P:(b + 1) * P], ones[:, 0:1],
                                          start=True, stop=True)
                mm.then_inc(a_ssum, 1)

            def spread(n):
                pe.wait_ge(a_rs, n + 1)
                for b in range(TB):
                    t = on_all_partitions(flat(6)[:, b * P:(b + 1) * P], small[:, 24 + b:25 + b])
                t.then_inc(a_bc, 1)

            def scores(g, i):
                h, c = divmod(i, CLASSES)
                if i == 0:
                    pe.wait_ge(a_rope, 10 * g + 10)
                else:
                    pe.wait_ge(a_m, 8 * g + i)
                q = a_q[:, c * 256 + h * P:c * 256 + (h + 1) * P]
                edge = P if h == 0 else P - EDGE
                nc.tensor.matmul(ps[:, 4, :], q, by_class(a_k)[:, :, h * P:(h + 1) * P], start=True, stop=True)
                nc.tensor.matmul(ps[:, 5, 0:CLASSES * EDGE], q, by_class(a_k)[:, :, edge:edge + EDGE],
                                 start=True, stop=True)
                nc.tensor.matmul(ps[:, 5, CLASSES * EDGE:MASK_B], q,
                                 a_k[:, c * 256 + (1 - h) * P:c * 256 + (2 - h) * P], start=True, stop=True
                                 ).then_inc(a_s, 1)

            def prob_transposes(g, i):
                pe.wait_ge(a_p, 8 * g + i + 1)
                if i == 0:
                    pe.wait_ge(a_va, g + 1)
                    pe.wait_ge(a_vd, 2 * g + 2)
                else:
                    pe.wait_ge(a_ta, 8 * g + i)
                    pe.wait_ge(a_td, 8 * g + i)
                transposes(lambda b: prob[:, i % 2, b * P:(b + 1) * P], 2, 4, a_t)
                nc.tensor.transpose(ps[:, 3, 0:P], prob[:, i % 2, KEYS - P:KEYS], ident[:])
                nc.tensor.transpose(ps[0:CLASSES * EDGE, 3, P:2 * P], prob[:, i % 2, 4 * P:KEYS - P], ident[:]
                                    ).then_inc(a_t, 1)

            def values(g, j):
                h, c = j // 2, 2 * (j % 2)
                pe.wait_ge(a_ta, 8 * g + 2 * j + 2)
                pe.wait_ge(a_td, 8 * g + 2 * j + 2)
                if j >= 2:
                    pe.wait_ge(a_y, 4 * g + j - 1)
                out = ps[:, 6 + j % 2, 0:256]
                for b in range(4):
                    nc.tensor.matmul(out, vtok[:, 4 * h + b, :], pT[:, b, :], start=b == 0, stop=False)
                for t in range(2):
                    nc.tensor.matmul(out[:, t * P:(t + 1) * P], vtok[:, 4 * (1 - h) + c + t, :],
                                     pT[:, 4, t * P:(t + 1) * P], start=False, stop=False, skip_group_check=True)
                nc.tensor.matmul(out, vedge[0:CLASSES * EDGE, h, :], pT[0:CLASSES * EDGE, 5, :], start=False, stop=True
                                 ).then_inc(a_pv, 1)

            def value_transposes(h):
                pe.wait_ge(proj_free, tile_out(h * A_TILES + A_TILE))
                if not (isinstance(h, int) and h == 0):
                    pe.wait_ge(a_ta, 8 * h)
                    pe.wait_ge(a_td, 8 * h)
                pe.wait_ge(a_vcut, h + 1)
                transposes(lambda b: a_v[:, (b % 4) * 256 + (b // 4) * P:(b % 4) * 256 + (b // 4 + 1) * P], 2, TB, a_vtr)
                for half in range(2):
                    t = nc.tensor.transpose(ps[0:CLASSES * EDGE, 4, half * P:(half + 1) * P],
                                            vcut[:, 1 - half].rearrange("p r n -> p (r n)"), ident[:])
                t.then_inc(a_vtr, 1)

            def attention_units(g, x):
                if x == 1:
                    square_sums(2 * g + 1)
                if x == 2:
                    spread(2 * g + 1)
                i = x - FIRST_TURN
                if i >= 2 and i % 2 == 0 and i <= 8:
                    values(g, i // 2 - 1)
                if 0 <= i < 8:
                    prob_transposes(g, i)
                if 0 <= x - FIRST_SCORES < 8:
                    scores(g, x - FIRST_SCORES)

            def attention_pe(h, first):
                def unit(x):
                    if first and x in (3, 5):
                        m_output_transposes(M_HEADS - 1, (x - 3) // 2)
                    if not first:
                        attention_units(h - 1, x)
                    if x == 17:
                        if not first:
                            pe.wait_ge(a_m, 8 * h)
                        square_sums(2 * h)
                    if x == 18:
                        value_transposes(h)
                    if x == 19:
                        if not first:
                            pe.wait_ge(a_y, 4 * h)
                        spread(2 * h)
                for u in range(A_PIECES):
                    piece(pe, h * A_TILES + A_TILE + u // PIECES, u % PIECES, lambda i: unit(2 * u + i))

            attention_pe(0, True)
            with pe.Fori(1, ATT_HEADS) as h:
                attention_pe(h, False)

            for u in range(A_PIECES):
                piece(pe, Z_TILE + u // PIECES, u % PIECES, lambda i: attention_units(ATT_HEADS - 1, 2 * u + i))
            with pe.Fori(Z_TILE + A_TILES, O_TILE) as tile:
                for s in range(PIECES):
                    piece(pe, tile, s)

            def y_made(kt):
                pe.wait_ge(o_lo, kt + 1)
            for s in range(PIECES):
                piece(pe, O_TILE, s, per_block=y_made)
            with pe.Fori(O_TILE + 1, O_TILE + O_TILES) as tile:
                for s in range(PIECES):
                    piece(pe, tile, s)

        @block.scalar
        def _(act):
            act.wait_ge(prep, 2)
            def ahead(piece_at):
                tile, s = piece_at
                weight_hi(act, tile + (s + LEAD) // PIECES, (s + LEAD) % PIECES)

            for kt in range(KT):
                act.wait_ge(x_in[kt], 16)
                if kt % 2 == 0:
                    nc.scalar.activation(h_hi[:, kt, :], x_raw[:, kt, :], ACT.Copy, scale=ncol[:, kt:kt + 1]
                                         ).then_inc(h_hid, 1)
                if kt >= SQ_RING:
                    act.wait_ge(x_sum, (kt - SQ_RING) // 2 + 1)
                nc.scalar.activation(xsq[:, kt % SQ_RING, :], x_raw[:, kt, :], ACT.Square).then_inc(x_sq, 1)
                if kt < LEAD:
                    weight_hi(act, 0, kt)
                if kt in AHEAD_OF_GATES:
                    ahead((0, AHEAD_OF_GATES.index(kt)))
            for s in range(len(AHEAD_OF_GATES), PIECES):
                ahead((0, s))

            read_out(act, 0, lambda i: nc.scalar.copy(gr[0][:, i * HALF:(i + 1) * HALF], psP[:, i, :]))
            act.wait_ge(x_sum, KT // 2)
            nc.scalar.activation(small[:, 16:24], ps[:, 5, 0:TB], ACT.Sqrt, bias=vec[:, 4:5], scale=1.0 / D_MODEL
                                 ).then_inc(x_rms, 1)

            def gate_rows():
                act.wait_ge(g_dve, GD_SPLIT)
                nc.scalar.activation(gr[4][0:64, :], gr[2][0:64, :], ACT.Abs).then_inc(g_act, 1)
                act.wait_ge(g_act, 1)
                nc.scalar.activation(gr[4][0:64, :], gr[4][0:64, :], ACT.Exp, scale=-1.0).then_inc(g_act, 1)
                act.wait_ge(g_act, 2)
                nc.scalar.activation(gr[4][0:64, :], gr[4][0:64, :], ACT.Ln, bias=1.0).then_inc(g_act, 1)

            def inter_weights():
                act.wait_ge(g_dve, GD_INTER)
                nc.scalar.activation(gr[5][0:64, :], gr[5][0:64, :], ACT.Exp).then_inc(g_act, 1)

            def gate_cols():
                act.wait_ge(g_pe, 1)
                for d in range(2):
                    src = ps[:, 5, :].rearrange("p (c r) -> p c r", r=64)[:, :, 32 * d:32 * d + M_HEADS]
                    nc.scalar.activation(e_cols[:, :, d, :], src, ACT.Exp, scale=-1.0).then_inc(g_act, 1)

            def m_step(j, n):
                c, d, i = chunk_of(n), n // TB, n % 2
                act.wait_ge(m_t, 16 * j + n + 1)
                if n >= 2 or not isinstance(j, int) or j > 0:
                    act.wait_ge(m_upd, 16 * j + n - 1)
                nc.scalar.activation(chunkbuf[:, i, 0, :], chunkbuf[:, i, 0, :], ACT.Exp, bias=gc[:, c, d:d + 1]
                                     ).then_inc(m_w, 1)
                act.wait_ge(m_w, 16 * j + n + 1)
                end = 0 if d else P - 1
                nc.scalar.activation(chunkbuf[:, i, 3, :], ps[:, 7, 0:P], ACT.Copy,
                                     scale=chunkbuf[:, i, 0, end:end + 1]).then_inc(m_kw, 1)

            def apply(tile, at, func):
                act.wait_ge(proj_free, tile_out(tile))
                return nc.scalar.activation(at, at, func)

            def mlstm_act(j, first):
                tile0 = j * M_TILES + G_TILE
                for u in range(M_PIECES):
                    ahead((tile0 + u // PIECES, u % PIECES))
                    if first and u == 1:
                        gate_rows()
                    if first and u == GATE_STEPS[4]:
                        inter_weights()
                    if first and u == GATE_STEPS[-1] + 1:
                        gate_cols()
                    if not first and u == 0:
                        m_square_sums(j - 1)
                    if u in (4, 8):
                        half = u // 4 - 1
                        act.wait_ge(m_vtr, 4 * j + 2 * half + 1)
                        nc.scalar.copy(v1[:, 0:4, half * P:(half + 1) * P], ps[:, 2, :].rearrange("p (b d) -> p b d", d=P)
                                       ).then_inc(m_va, 1)
                    if u in (20, 24):
                        e = u // 4 - 5
                        apply(tile0 + 4 + e, gate[:, e * SEQ:(e + 1) * SEQ], ACT.Sigmoid).then_inc(m_act, 1)
                    if u == 28:
                        apply(tile0 + 6, vst[:], ACT.Silu).then_inc(m_act, 1)
                    if 15 <= u < 31:
                        m_step(j, u - 15)
                    if u == 31:
                        apply(tile0 + 7, vst[:], ACT.Silu).then_inc(m_act, 1)

            def m_square_sums(j):
                for c in range(TB):
                    if c == 0:
                        act.wait_ge(m_h, 16 * j + 16)
                    nc.scalar.activation(chunkbuf[:, 0, 0:2, :].rearrange("p k t -> p (k t)"),
                                         hbuf[:, c * 256:(c + 1) * 256], ACT.Square,
                                         accum_out=small[:, 16 + c:17 + c]).then_inc(m_ss, 1)
                    act.wait_ge(m_ss, 8 * j + c + 1)
                nc.scalar.activation(small[:, 24:32], small[:, 16:24], ACT.Sqrt, bias=vec[:, 4:5], scale=1.0 / 256
                                     ).then_inc(m_rms, 1)

            mlstm_act(0, True)
            with act.Fori(1, M_HEADS) as j:
                mlstm_act(j, False)

            def squares(n, src):
                nc.scalar.activation(prob[:, 0, :], src, ACT.Square).then_inc(a_sq, 1)

            def root(n):
                act.wait_ge(a_ssum, n + 1)
                nc.scalar.activation(small[:, 16:24], ps[:, 5, 0:TB], ACT.Sqrt, bias=vec[:, 4:5], scale=1.0 / P
                                     ).then_inc(a_rms, 1)

            def exponentials(g, i):
                act.wait_ge(a_m, 8 * g + i + 1)
                nc.scalar.activation(prob[:, i % 2, 0:KEYS], prob[:, i % 2, 0:KEYS], ACT.Exp,
                                     bias=small[:, i % 2:i % 2 + 1], scale=-1.0,
                                     accum_out=small[:, 2 + i % 2:3 + i % 2]).then_inc(a_e, 1)

            def take_probs(g, i):
                act.wait_ge(a_t, 16 * g + 2 * i + 1)
                if i == 0:
                    act.wait_ge(a_rope, 10 * g + 10)
                if i % 2 == 0 and i > 0:
                    act.wait_ge(a_pv, 4 * g + i // 2)
                nc.scalar.copy(pT[:, 0:4, (i % 2) * P:(i % 2 + 1) * P], ps[:, 2, :].rearrange("p (b q) -> p b q", q=P)
                               ).then_inc(a_ta, 1)

            def attention_ops(g, x):
                if x == 0:
                    act.wait_ge(a_ssum, 2 * g + 1)
                    act.wait_ge(proj_free, tile_out(g * A_TILES + A_TILE + 2))
                    squares(2 * g + 1, a_k[:])
                if x == 1:
                    root(2 * g + 1)
                if 0 <= x - FIRST_TURN < 8:
                    take_probs(g, x - FIRST_TURN)
                if 0 <= x - FIRST_SCORES < 8:
                    exponentials(g, x - FIRST_SCORES)

            def attention_act(h, first):
                tile0 = h * A_TILES + A_TILE
                for x in range(2 * A_PIECES):
                    if x % 2 == 0:
                        u = x // 2
                        ahead((tile0 + u // PIECES, u % PIECES))
                    if first and x == 0:
                        m_square_sums(M_HEADS - 1)
                    if not first:
                        attention_ops(h - 1, x)
                    if x == 8:
                        act.wait_ge(proj_free, tile_out(tile0))
                        nc.scalar.copy(vcut.rearrange("p e r n -> p r e n"),
                                       by_class(a_v)[:, :, P - EDGE:P + EDGE].rearrange("p r (e n) -> p r e n", e=2)
                                       ).then_inc(a_vcut, 1)
                    if x == 16:
                        if not first:
                            act.wait_ge(a_t, 16 * h - 2)
                        else:
                            act.wait_ge(m_out, 16 * M_HEADS)
                        act.wait_ge(proj_free, tile_out(tile0 + 1))
                        squares(2 * h, a_q[:])
                    if x == 17:
                        root(2 * h)
                    if x == 18:
                        act.wait_ge(a_vtr, 3 * h + 1)
                        if not first:
                            act.wait_ge(a_pv, 4 * h)
                        nc.scalar.copy(vtok[:, 0:4, :], ps[:, 2, :].rearrange("p (b d) -> p b d", d=P)
                                       ).then_inc(a_va, 1)

            attention_act(0, True)
            with act.Fori(1, ATT_HEADS) as h:
                attention_act(h, False)

            def z_silu(t):
                apply(Z_TILE + t, zs[:, t * SEQ:(t + 1) * SEQ], ACT.Silu).then_inc(z_act, 1)

            for x in range(2 * A_PIECES):
                if x % 2 == 0:
                    ahead((Z_TILE + x // 2 // PIECES, x // 2 % PIECES))
                attention_ops(ATT_HEADS - 1, x)
                if x in (8, 16):
                    z_silu(x // 8 - 1)
            for t in range(A_TILES, ATT_HEADS):
                for s in range(PIECES):
                    ahead((Z_TILE + t, s))
                    if s == 0:
                        z_silu(t - 1)
            z_silu(ATT_HEADS - 1)

            for kt in range(KT):
                n = kt // 2
                if kt % 2 == 0:
                    act.wait_ge(z_y, n + 1)
                    src = zs[:, n * SEQ:(n + 1) * SEQ]
                else:
                    act.wait_ge(z_in[n % 4], 16 * ((8 + n) // 4 + 1))
                    src = yring[:, n % 4, :]
                if kt == 0:
                    act.wait_ge(w_used, O_PIECE)
                nc.scalar.copy(h_hi[:, kt, :], src).then_inc(o_hi, 1)
            for s in range(PIECES):
                ahead((O_TILE, s))
            with act.Fori(O_TILE + 1, O_TILE + O_TILES - 1) as tile:
                for s in range(PIECES):
                    ahead((tile, s))
            for s in range(PIECES - LEAD):
                ahead((O_TILE + O_TILES - 1, s))

        @block.vector
        def _(dve):
            nc.vector.memset(ones[:], 1.0).then_inc(ones_set, 1)
            dve.wait_ge(consts, 80)
            nc.vector.tensor_scalar(vec[:, 3:4], vec[:, 0:1], -float(P) ** -0.5, None, ALU.mult).then_inc(prep, 1)
            nc.vector.memset(vec[:, 4:5], EPS).then_inc(prep, 1)
            def ahead(piece_at):
                tile, s = piece_at
                weight_lo(dve, tile + (s + LEAD) // PIECES, (s + LEAD) % PIECES)

            for kt in range(KT):
                hi_of = h_hi[:, kt, :].bitcast(F32)
                if kt % 2 == 1:
                    dve.wait_ge(x_in[kt], 16)
                    nc.vector.tensor_scalar(h_hi[:, kt, :], x_raw[:, kt, :], ncol[:, kt:kt + 1], None, ALU.mult
                                            ).then_inc(h_hiv, 1)
                    dve.wait_ge(h_hiv, kt // 2 + 1)
                else:
                    dve.wait_ge(h_hid, kt // 2 + 1)
                dve.wait_ge(x_sq, kt + 1)
                nc.vector.scalar_tensor_tensor(h_lo[:, kt, :], x_raw[:, kt, :], ncol[:, kt:kt + 1], hi_of,
                                               ALU.mult, ALU.subtract).then_inc(h_lod, 1)
                if kt < LEAD:
                    weight_lo(dve, 0, kt)
                if kt in AHEAD_OF_GATES:
                    ahead((0, AHEAD_OF_GATES.index(kt)))
            for s in range(len(AHEAD_OF_GATES), PIECES):
                ahead((0, s))
            dve.wait_ge(x_rms, 1)
            nc.vector.reciprocal(small[:, 24:32], small[:, 16:24]).then_inc(x_rs, 1)
            nc.vector.memset(v1[:, :, 256:258], 1.0).then_inc(prep, 1)

            def halves(out, scale=1.0):
                return lambda i: nc.vector.scalar_tensor_tensor(
                    out[:, i * HALF:(i + 1) * HALF], psP[:, i, :], scale, xrs[:, i * HALF:(i + 1) * HALF],
                    ALU.mult, ALU.mult)

            def halves_by_class(out):
                def as_classes(row):
                    return row.rearrange("p (n r) -> p r n", r=CLASSES)
                return lambda i: nc.vector.tensor_tensor(
                    by_class(out)[:, :, i * P:(i + 1) * P], as_classes(psP[:, i, :]),
                    as_classes(xrs[:, i * HALF:(i + 1) * HALF]), ALU.mult)

            count = [0]

            def g_step(ins):
                ins.then_inc(g_dve, 1)
                count[0] += 1
                dve.wait_ge(g_dve, count[0])

            def gate_rows(part):
                raw, li, f, m, t, wi = gr
                if part == 0:
                    dve.wait_ge(x_bc, 1)
                    nc.vector.tensor_copy(xrs[:], flat(6)).then_inc(x_norm, 1)
                    dve.wait_ge(proj_free, tile_out(0))
                    dve.wait_ge(x_norm, 1)
                    g_step(nc.vector.tensor_tensor(raw[:], raw[:], xrs[:], ALU.mult))
                    g_step(nc.vector.tensor_scalar(raw[:], raw[:], vec[:, 2:3], None, ALU.add))
                    g_step(nc.vector.tensor_copy(li[0:32, :], raw[0:32, :]))
                    g_step(nc.vector.tensor_copy(li[32:64, :], raw[32:64, ::-1]))
                    g_step(nc.vector.tensor_copy(f[0:32, :], raw[64:96, :]))
                    g_step(nc.vector.tensor_copy(f[32:64, :], raw[96:128, ::-1]))
                    assert count[0] == GD_SPLIT
                if part == 1:
                    dve.wait_ge(g_act, 3)
                    g_step(nc.vector.scalar_tensor_tensor(f[0:64, :], f[0:64, :], 0.0, t[0:64, :],
                                                          ALU.min, ALU.subtract))
                    g_step(nc.vector.tensor_tensor_scan(out=m[0:64, :], data0=f[0:64, :], data1=li[0:64, :], initial=NEG,
                                                        op0=ALU.add, op1=ALU.max))
                    g_step(nc.vector.memset(t[0:64, :], 0.0))
                if part == 2:
                    for c in range(TB):
                        cols = slice(c * P, (c + 1) * P)
                        g_step(nc.vector.tensor_tensor_scan(out=raw[0:64, cols], data0=f[0:64, cols],
                                                            data1=t[0:64, cols], initial=0.0, op0=ALU.add, op1=ALU.add))
                    g_step(nc.vector.tensor_tensor(f[0:64, :], li[0:64, :], raw[0:64, :], ALU.subtract))
                    g_step(nc.vector.tensor_tensor(t[0:64, :], raw[0:64, :], m[0:64, :], ALU.subtract))
                if part == 3:
                    g_step(nc.vector.tensor_scalar(wi[0:64, 0:P], t[0:64, 0:P], NEG, None, ALU.add))
                    for c in range(1, TB):
                        g_step(nc.vector.tensor_scalar(wi[0:64, c * P:(c + 1) * P], t[0:64, c * P:(c + 1) * P],
                                                       m[0:64, c * P - 1:c * P], None, ALU.add))
                    assert count[0] == GD_INTER
                    g_step(nc.vector.tensor_copy(rows[0:32, :], t[0:32, :]))
                    g_step(nc.vector.tensor_copy(rows[32:64, :], t[32:64, ::-1]))
                if part == 4:
                    g_step(nc.vector.tensor_copy(li[0:32, :], m[0:32, :]))
                    g_step(nc.vector.tensor_copy(li[32:64, :], m[32:64, ::-1]))
                    g_step(nc.vector.tensor_copy(m[0:32, :], f[0:32, :]))
                    g_step(nc.vector.tensor_copy(m[32:64, :], f[32:64, ::-1]))
                    dve.wait_ge(g_act, 4)
                    g_step(nc.vector.tensor_copy(rows[64:96, :], wi[0:32, :]))
                    g_step(nc.vector.tensor_copy(rows[96:128, :], wi[32:64, ::-1]))
                    assert count[0] == GD_ROWS

            def gate_cols():
                dve.wait_ge(g_pe, 1)
                for d in range(2):
                    src = ps[:, 4, :].rearrange("p (c r) -> p c r", r=64)[:, :, 32 * d:32 * d + M_HEADS]
                    g_step(nc.vector.tensor_copy(g_cols[:, :, d, :], src))
                for k in range(4):
                    src = flat(6).rearrange("p (c r) -> p c r", r=P)[:, :, 32 * k:32 * k + M_HEADS]
                    g_step(nc.vector.tensor_copy(a_cols[:, :, k, :], src))

            def m_mask(j, n):
                d, i = n // TB, n % 2
                dve.wait_ge(m_x, 16 * j + n + 1)
                if n >= 2 or not isinstance(j, int) or j > 0:
                    dve.wait_ge(m_kw, 16 * j + n - 1)
                    dve.wait_ge(m_num, 16 * j + n - 1)
                    dve.wait_ge(m_ops, 16 * j + n - 1)
                nc.vector.tensor_tensor(chunkbuf[:, i, 0, :], ps[:, 6, 0:P], tri_m[:, d, :], ALU.add).then_inc(m_t, 1)

            def m_operands(j, n):
                c, d, i = chunk_of(n), n // TB, n % 2
                end = 0 if d else P - 1
                nc.vector.tensor_tensor(chunkbuf[:, i, 2, :], qT[:, c * P:(c + 1) * P], ps[:, 6, P:2 * P], ALU.mult)
                if n >= 2 or not isinstance(j, int) or j > 0:
                    dve.wait_ge(m_c, 16 * j + n - 1)
                nc.vector.tensor_copy(small[:, 8 + i:9 + i], ps[:, 6, P + end:P + end + 1])
                dve.wait_ge(m_w, 16 * j + n + 1)
                nc.vector.tensor_tensor(chunkbuf[:, i, 1, :], ps[:, 6, 2 * P:3 * P], chunkbuf[:, i, 0, :], ALU.mult
                                        ).then_inc(m_ops, 1)

            def m_results(j, n):
                c, d, i = chunk_of(n), n // TB, n % 2
                dve.wait_ge(m_upd, 16 * j + n + 1)
                after = cst[:, (n + 1) % 2, 0:MV]
                if n % TB == 0:
                    nc.vector.tensor_copy(after, ps[:, 5, 0:MV]).then_inc(m_c, 1)
                else:
                    dve.wait_ge(m_c, 16 * j + n)
                    nc.vector.scalar_tensor_tensor(after, cst[:, n % 2, 0:MV], small[:, 8 + i:9 + i], ps[:, 5, 0:MV],
                                                   ALU.mult, ALU.add).then_inc(m_c, 1)
                den = ps[:, 4, 256:257]
                nc.vector.tensor_scalar(small[:, 10:11], den, ec[:, c, d:d + 1], None, ALU.max).then_inc(m_den, 1)
                dve.wait_ge(m_den, 48 * j + 3 * n + 1)
                nc.vector.scalar_tensor_tensor(small[:, 11:12], den, -1.0, small[:, 10:11], ALU.mult, ALU.max
                                               ).then_inc(m_den, 1)
                dve.wait_ge(m_den, 48 * j + 3 * n + 2)
                nc.vector.reciprocal(small[:, 12:13], small[:, 11:12]).then_inc(m_den, 1)
                dve.wait_ge(m_den, 48 * j + 3 * n + 3)
                h_at = hbuf[:, c * 256:(c + 1) * 256]
                if d == 0:
                    nc.vector.tensor_scalar(h_at, ps[:, 4, 0:256], small[:, 12:13], None, ALU.mult).then_inc(m_h, 1)
                else:
                    if n == TB:
                        dve.wait_ge(m_h, 16 * j + n)
                    nc.vector.scalar_tensor_tensor(h_at, ps[:, 4, 0:256], small[:, 12:13], h_at, ALU.mult, ALU.add
                                                   ).then_inc(m_h, 1)

            def m_normalise(j):
                dve.wait_ge(m_rms, j + 1)
                nc.vector.reciprocal(small[:, 32:40], small[:, 24:32]).then_inc(m_rs, 1)
                dve.wait_ge(m_rs, j + 1)
                for c in range(TB):
                    nc.vector.tensor_scalar(hbuf[:, c * 256:(c + 1) * 256], hbuf[:, c * 256:(c + 1) * 256],
                                            small[:, 32 + c:33 + c], None, ALU.mult).then_inc(m_hn, 1)

            def m_outputs(j, e):
                for b in range(2):
                    dve.wait_ge(m_htr, 4 * j + 2 * e + b + 1)
                    at = gate[:, e * SEQ + b * HALF:e * SEQ + (b + 1) * HALF]
                    nc.vector.tensor_tensor(at, ps[:, 2 + b, :], at, ALU.mult).then_inc(m_y, 1)

            def mlstm_dve(j, first):
                tile0 = j * M_TILES + G_TILE
                for u in range(M_PIECES):
                    ahead((tile0 + u // PIECES, u % PIECES))
                    if u % PIECES == PIECES - 1:
                        m_read_out(j, tile0, u // PIECES, first)
                    if first and u in GATE_STEPS:
                        gate_rows(GATE_STEPS.index(u))
                    if first and u == GATE_STEPS[-1] + 1:
                        gate_cols()
                    if not first:
                        if u == 0:
                            m_gates(j - 1, 1)
                            m_normalise(j - 1)
                        if u in (1, 2):
                            m_outputs(j - 1, u - 1)
                    if u in (4, 8):
                        half = u // 4 - 1
                        dve.wait_ge(m_vtr, 4 * j + 2 * half + 2)
                        nc.vector.tensor_copy(v1[:, 4:8, half * P:(half + 1) * P],
                                              ps[:, 3, :].rearrange("p (b d) -> p b d", d=P)).then_inc(m_vd, 1)
                    if u == 29:
                        m_gates(j, 0)
                    if u >= 16:
                        m_results(j, u - 16)
                    if 15 <= u < 31:
                        m_mask(j, u - 15)
                        m_operands(j, u - 15)

            def m_read_out(j, tile0, k, first):
                if k == 0 and not first:
                    dve.wait_ge(m_g, 2 * j)
                if k == 1:
                    dve.wait_ge(m_vtr, 4 * j + 2)
                if k == 2 and first:
                    dve.wait_ge(g_pe, 1)
                if k in (4, 5) and not first:
                    dve.wait_ge(m_out, 16 * j)
                if k == 6:
                    dve.wait_ge(m_vtr, 4 * j + 4)
                if k == 7:
                    dve.wait_ge(m_g, 2 * j + 1)
                out = (vst, vst, kT, qT, gate[:, 0:SEQ], gate[:, SEQ:2 * SEQ], vst, vst)[k]
                read_out(dve, tile0 + k, halves(out, float(P) ** -0.5 if k == 2 else 1.0))

            def m_gates(j, e):
                dve.wait_ge(m_act, 4 * j + 3 + e)
                at = gate[:, e * SEQ:(e + 1) * SEQ]
                nc.vector.scalar_tensor_tensor(at, vst[:], mw[:, e:e + 1], at, ALU.mult, ALU.mult).then_inc(m_g, 1)

            mw = small[:, 40:42]
            mlstm_dve(0, True)
            with dve.Fori(1, M_HEADS) as j:
                mlstm_dve(j, False)

            def reciprocal_rms(n):
                dve.wait_ge(a_rms, n + 1)
                if not (isinstance(n, int) and n == 0):
                    dve.wait_ge(a_bc, n)
                nc.vector.reciprocal(small[:, 24:32], small[:, 16:24]).then_inc(a_rs, 1)

            def rotate(n, qk, w, part):
                at, tmp = 5 * n, prob[:, 1, :]
                if part == 0:
                    dve.wait_ge(a_bc, n + 1)
                    nc.vector.scalar_tensor_tensor(qk, qk, w, flat(6), ALU.mult, ALU.mult).then_inc(a_rope, 1)
                if part == 1:
                    dve.wait_ge(a_rope, at + 1)
                    nc.vector.memset(small[:, 48:49], 0.0)
                    nc.vector.stream_shuffle(tmp[0:ROT, :], qk[0:ROT, :], mask=[(r + ROT // 2) % ROT for r in range(ROT)]
                                             ).then_inc(a_rope, 1)
                    dve.wait_ge(a_rope, at + 2)
                    nc.vector.tensor_tensor(tmp[0:ROT, :], tmp[0:ROT, :], sin[0:ROT, :], ALU.mult).then_inc(a_rope, 1)
                if part == 2:
                    nc.vector.tensor_tensor(qk[0:ROT, :], qk[0:ROT, :], cos[0:ROT, :], ALU.mult).then_inc(a_rope, 1)
                    dve.wait_ge(a_rope, at + 4)
                    nc.vector.tensor_tensor(qk[0:ROT, :], qk[0:ROT, :], tmp[0:ROT, :], ALU.add).then_inc(a_rope, 1)

            def masked(g, i):
                h, c = divmod(i, CLASSES)
                dve.wait_ge(a_s, 8 * g + i + 1)
                if i >= 2:
                    dve.wait_ge(a_t, 16 * g + 2 * i - 2)
                nc.vector.memset(small[:, 48:49], 0.0)
                at = P * (CLASSES - 1 - c)
                nc.vector.tensor_tensor_reduce(prob[:, i % 2, 0:4 * P], psS[:, 0:4 * P], mask_a[:, at:at + 4 * P], 1.0,
                                               -3 * NEG, ALU.add, ALU.min, small[:, 6 + i % 2:7 + i % 2]
                                               ).then_inc(a_mh, 1)
                dve.wait_ge(a_mh, 8 * g + i + 1)
                nc.vector.memset(small[:, 48:49], 0.0)
                nc.vector.tensor_tensor_reduce(prob[:, i % 2, 4 * P:KEYS], psS[:, 4 * P:KEYS], mask_b[:, i, :], 1.0,
                                               small[:, 6 + i % 2:7 + i % 2], ALU.add, ALU.min,
                                               small[:, i % 2:i % 2 + 1]).then_inc(a_m, 1)

            def normalised(g, i):
                dve.wait_ge(a_e, 8 * g + i + 1)
                nc.vector.reciprocal(small[:, 4 + i % 2:5 + i % 2], small[:, 2 + i % 2:3 + i % 2]).then_inc(a_r, 1)
                dve.wait_ge(a_r, 8 * g + i + 1)
                nc.vector.tensor_scalar(prob[:, i % 2, 0:KEYS], prob[:, i % 2, 0:KEYS],
                                        small[:, 4 + i % 2:5 + i % 2], None, ALU.mult).then_inc(a_p, 1)

            def attention_ops(g, x):
                if x == 1:
                    reciprocal_rms(2 * g + 1)
                if x in (2, 3, 4):
                    rotate(2 * g + 1, a_k, vec[:, 1:2], x - 2)
                if 0 <= x - FIRST_SCORES - 1 < 8:
                    normalised(g, x - FIRST_SCORES - 1)
                i = x - FIRST_TURN
                if 0 <= i < 8:
                    dve.wait_ge(a_t, 16 * g + 2 * i + 2)
                    if i == 0:
                        dve.wait_ge(a_rope, 10 * g + 10)
                    if i % 2 == 0 and i > 0:
                        dve.wait_ge(a_pv, 4 * g + i // 2)
                    nc.vector.tensor_copy(pT[:, 4:6, (i % 2) * P:(i % 2 + 1) * P],
                                          ps[:, 3, 0:256].rearrange("p (b q) -> p b q", q=P)).then_inc(a_td, 1)
                if 0 <= x - FIRST_SCORES < 8:
                    masked(g, x - FIRST_SCORES)
                if i >= 2 and i % 2 == 0 and i <= 8:
                    j = i // 2 - 1
                    h, c = j // 2, 2 * (j % 2)
                    dve.wait_ge(a_pv, 4 * g + j + 1)
                    if j == 0:
                        dve.wait_ge(a_out, 16 * (g + 1))
                    nc.vector.tensor_copy(
                        ystage.rearrange("p (n r) -> p r n", r=CLASSES)[:, c:c + 2, h * P:(h + 1) * P],
                        ps[:, 6 + j % 2, 0:256].rearrange("p (r n) -> p r n", n=P)).then_inc(a_y, 1)

            def attention_dve(h, first):
                tile0 = h * A_TILES + A_TILE
                for x in range(2 * A_PIECES):
                    if x % 2 == 0:
                        u = x // 2
                        ahead((tile0 + u // PIECES, u % PIECES))
                    if first and x == 0:
                        m_gates(M_HEADS - 1, 1)
                        m_normalise(M_HEADS - 1)
                    if first and x in (3, 5):
                        m_outputs(M_HEADS - 1, (x - 3) // 2)
                    if x == 7:
                        if not first:
                            dve.wait_ge(a_vtr, 3 * h)
                        read_out(dve, tile0, halves_by_class(a_v))
                    if x == 15:
                        if not first:
                            dve.wait_ge(a_s, 8 * h)
                        read_out(dve, tile0 + 1, halves_by_class(a_q))
                    if not first:
                        attention_ops(h - 1, x)
                    if x == 23:
                        read_out(dve, tile0 + 2, halves_by_class(a_k))
                    if x == 17:
                        reciprocal_rms(2 * h)
                    if x == 18:
                        dve.wait_ge(a_vtr, 3 * h + 2)
                        nc.vector.tensor_copy(vtok[:, 4:8, :], ps[:, 3, :].rearrange("p (b d) -> p b d", d=P)
                                              ).then_inc(a_vd, 1)
                        dve.wait_ge(a_vtr, 3 * h + 3)
                        nc.vector.tensor_copy(vedge[0:CLASSES * EDGE],
                                              ps[0:CLASSES * EDGE, 4, 0:256].rearrange("p (h d) -> p h d", d=P)
                                              ).then_inc(a_vd, 1)
                    if x in (19, 20, 21):
                        if x == 20:
                            dve.wait_ge(a_cs, 32 * h + 32)
                            if not first:
                                dve.wait_ge(a_t, 16 * h)
                        rotate(2 * h, a_q, vec[:, 3:4], x - 19)

            attention_dve(0, True)
            with dve.Fori(1, ATT_HEADS) as h:
                attention_dve(h, False)

            def gated(t):
                dve.wait_ge(z_act, t + 1)
                dve.wait_ge(z_in[t % 4], 16 * (t // 4 + 1))
                at = zs[:, t * SEQ:(t + 1) * SEQ]
                nc.vector.tensor_tensor(at, at, yring[:, t % 4, :], ALU.mult).then_inc(z_y, 1)

            def z_read_out(t):
                if t == 0:
                    dve.wait_ge(a_vtr, 3 * ATT_HEADS)
                elif t < A_TILES:
                    dve.wait_ge(a_s, 8 * ATT_HEADS)
                if t == ATT_HEADS - 1:
                    dve.wait_ge(a_out, 16 * (ATT_HEADS + 1))
                read_out(dve, Z_TILE + t, halves(zs[:, t * SEQ:(t + 1) * SEQ]))

            for x in range(2 * A_PIECES):
                if x % 2 == 0:
                    ahead((Z_TILE + x // 2 // PIECES, x // 2 % PIECES))
                if x % 8 == 7:
                    z_read_out(x // 8)
                attention_ops(ATT_HEADS - 1, x)
            for t in range(A_TILES, ATT_HEADS):
                for s in range(PIECES):
                    ahead((Z_TILE + t, s))
                    if t == A_TILES and s >= 1:
                        gated(s - 1)
                    if t > A_TILES and s == 1:
                        gated(t - 1)
                z_read_out(t)
            gated(ATT_HEADS - 1)

            for kt in range(KT):
                n = kt // 2
                src = zs[:, n * SEQ:(n + 1) * SEQ] if kt % 2 == 0 else yring[:, n % 4, :]
                dve.wait_ge(o_hi, kt + 1)
                nc.vector.tensor_tensor(h_lo[:, kt, :], src, h_hi[:, kt, :].bitcast(F32), ALU.subtract
                                        ).then_inc(o_lo, 1)

            def output(tile, i, n2, first):
                dve.wait_ge(o_x[i], 16 * (n2 + 1))
                if not first:
                    dve.wait_ge(o_out[i], 16 * n2)
                read_out(dve, tile, lambda k: nc.vector.tensor_tensor(
                    oblk[:, i, k * HALF:(k + 1) * HALF], psP[:, k, :], xres[:, i, k * HALF:(k + 1) * HALF], ALU.add))

            for i in range(2):
                for s in range(PIECES):
                    ahead((O_TILE + i, s))
                if i == 0:
                    dve.wait_ge(o_lo, KT)
                output(O_TILE + i, i, 0, True)
            with dve.Fori(1, O_TILES // 2 - 1) as n2:
                for i in range(2):
                    for s in range(PIECES):
                        ahead((n2 * 2 + O_TILE + i, s))
                    output(n2 * 2 + O_TILE + i, i, n2, False)
            last = O_TILES // 2 - 1
            for i in range(2):
                for s in range(PIECES if i == 0 else PIECES - LEAD):
                    ahead((O_TILE + 2 * last + i, s))
                output(O_TILE + 2 * last + i, i, last, False)

        @block.gpsimd
        def _(pool):
            pool.wait_ge(consts, 80)

            nc.gpsimd.memset(small[:, 50:51], 0.0).then_inc(p_held, 1)

            def held(k):
                pool.wait_ge(p_held, k + 1)
                nc.gpsimd.tensor_tensor(small[:, 51:52], small[:, 50:51], small[:, 50:51], ALU.add
                                        ).then_inc(p_held, 1)

            def select(j, first):
                if first:
                    pool.wait_ge(g_dve, GD_COLS)
                    pool.wait_ge(g_act, 6)
                    pool.wait_ge(prep, 3)
                else:
                    pool.wait_ge(m_h, 16 * j)
                    pool.wait_ge(m_g, 2 * j)
                at = 3 * j
                nc.gpsimd.tensor_copy(ac.rearrange("p c k d -> p c (k d)"),
                                      a_cols[:, :, :, bass.ds(j, 1)].rearrange("p c k h -> p c (k h)")
                                      ).then_inc(m_pick, 1)
                pool.wait_ge(m_pick, at + 1)
                nc.gpsimd.tensor_copy(gc[:], g_cols[:, :, :, bass.ds(j, 1)].rearrange("p c d h -> p c (d h)")
                                      ).then_inc(m_pick, 1)
                pool.wait_ge(m_pick, at + 2)
                nc.gpsimd.tensor_copy(small[:, 40:42], mcol[:, bass.ds(2 * j, 2)]).then_inc(m_pick, 1)
                pool.wait_ge(m_pick, at + 3)
                nc.gpsimd.tensor_copy(ec[:], e_cols[:, :, :, bass.ds(j, 1)].rearrange("p c d h -> p c (d h)")
                                      ).then_inc(m_sel, 1)

            def store_mlstm(j):
                pool.wait_ge(m_y, 4 * j + 4)
                if not isinstance(j, int):
                    held(j)
                pool.dma_start(y_dram[bass.ds(2 * j + ATT_HEADS, 2)].rearrange("e p t -> p e t"),
                               gate.rearrange("p (e t) -> p e t", e=2)).then_inc(m_out, 16)

            for k in range(KT // 2):
                pool.wait_ge(x_sq, 2 * k + 2)
                at = xsq[:, (2 * k + 1) % SQ_RING, :]
                nc.gpsimd.tensor_tensor(at, at, xsq[:, 2 * k % SQ_RING, :], ALU.add).then_inc(x_pair, 1)

            select(0, True)
            with pool.Fori(1, M_HEADS) as j:
                select(j, False)
                store_mlstm(j - 1)
            store_mlstm(M_HEADS - 1)
            pool.wait_ge(m_h, 16 * M_HEADS)
            pool.wait_ge(m_out, 16 * M_HEADS)
            pool.dma_start(view(5120, MASK_A + 8 * MASK_B), att_mask).then_inc(a_out, 16)

            def tables():
                pool.dma_start(cos[0:ROT, :], rope[0]).then_inc(a_cs, 16)
                pool.dma_start(sin[0:ROT, :], rope[1]).then_inc(a_cs, 16)

            def store_attention(h):
                pool.dma_start(y_dram[bass.ds(h, 1)].rearrange("e p t -> p (e t)"), ystage).then_inc(a_out, 16)

            tables()
            with pool.Fori(1, ATT_HEADS) as h:
                pool.wait_ge(a_pv, 4 * h)
                held(2 * h + M_HEADS - 3)
                tables()
                pool.wait_ge(a_y, 4 * h)
                held(2 * h + M_HEADS - 2)
                store_attention(h - 1)
            pool.wait_ge(a_y, 4 * ATT_HEADS)
            store_attention(ATT_HEADS - 1)

            pool.wait_ge(a_pv, 4 * ATT_HEADS)
            for n in range(ATT_HEADS + 2 * M_HEADS):
                if n == 0:
                    pool.wait_ge(a_out, 16 * (ATT_HEADS + 1))
                if n - 4 >= ATT_HEADS:
                    pool.wait_ge(o_lo, 2 * (n - 4 - ATT_HEADS) + 2)
                elif n >= 4:
                    pool.wait_ge(z_y, n - 3)
                pool.dma_start(yring[:, n % 4, :], y_dram[n]).then_inc(z_in[n % 4], 16)
            pool.wait_ge(o_lo, KT)
            for i in range(2):
                pool.dma_start(xres[:, i, :], xT[i]).then_inc(o_x[i], 16)
            with pool.Fori(0, O_TILES // 2 - 1) as n2:
                for i in range(2):
                    pool.wait_ge(proj_free, tile_out(n2 * 2 + O_TILE + i))
                    held(2 * n2 + M_HEADS - 1 + 2 * (ATT_HEADS - 1) + i)
                    pool.dma_start(outT[bass.ds(2 * n2 + i, 1)].rearrange("a p t -> p (a t)"), oblk[:, i, :]
                                   ).then_inc(o_out[i], 16)
                    pool.dma_start(xres[:, i, :], xT[bass.ds(2 * n2 + 2 + i, 1)].rearrange("a p t -> p (a t)")
                                   ).then_inc(o_x[i], 16)
            for i in range(2):
                pool.wait_ge(proj_free, tile_out(O_TILE + O_TILES - 2 + i))
                pool.dma_start(outT[O_TILES - 2 + i], oblk[:, i, :]).then_inc(o_out[i], 16)
            for i in range(2):
                pool.wait_ge(o_out[i], 16 * (O_TILES // 2))


GD_SPLIT = 6
GD_INTER = GD_SPLIT + 3 + TB + 2 + TB
GD_ROWS = GD_INTER + 8
GD_COLS = GD_ROWS + 6


def shape_constants():
    pos = np.arange(SEQ, dtype=np.float32)
    inv = (500000.0 ** (-np.arange(0, ROT, 2, dtype=np.float32) / ROT)).astype(np.float32)
    ang = (pos[:, None] * inv[None, :]).astype(np.float32).T
    c, s = np.cos(ang), np.sin(ang)
    rope = np.stack([np.concatenate([c, c]), np.concatenate([-s, s])]).astype(np.float32)
    rope = np.ascontiguousarray(rope.reshape(2, ROT, SEQ // CLASSES, CLASSES).transpose(0, 1, 3, 2)).reshape(2, ROT, SEQ)

    def entry(rel):
        n = np.zeros(rel.shape)
        for window, dil in ((128, 1), (512, 4), (2048, 16)):
            n += (rel % dil == 0) & (np.abs(rel) // dil <= window // (2 * dil))
        return np.where(n > 0, -np.log(np.maximum(n, 1)), -NEG)

    query, place = np.arange(P)[:, None], np.arange(P)[None, :]
    tables = [entry(4 * (place - query) + diff) for diff in range(1 - CLASSES, CLASSES)]
    for half in range(2):
        for own in range(CLASSES):
            for c in range(CLASSES):
                e = place[:, :EDGE] + (P if half == 0 else -EDGE)
                edge = entry(4 * (e - query) + c - own)
                tables.append(np.full_like(edge, -NEG) if c == own else edge)
            tables.append(entry(4 * (place + (P if half == 0 else -P) - query)))
    table = np.concatenate(tables, axis=1).astype(np.float32)
    s_, t_ = np.arange(P)[:, None], np.arange(P)[None, :]
    tri = np.stack([np.where(s_ <= t_, 0.0, NEG), np.where(s_ >= t_, 0.0, NEG)], axis=1).astype(np.float32)
    return rope, table, np.eye(P, dtype=np.float32), tri


def weight_pieces(w):
    n = w.shape[1] // P
    return w.reshape(PIECES, KP, P, n, P).transpose(3, 0, 2, 1, 4).reshape(n * PIECES, P, KP * P)


def kernel(x, norm_w, w_in, b_gates, q_norm_w, k_norm_w, m_norm_w, w_out):
    import numpy as _np
    import concourse.bacc as _bacc
    from concourse import mybir as _mybir
    from concourse.bass_utils import run_bass_kernel_spmd as _run

    x, norm_w, w_in, b_gates, q_norm_w, k_norm_w, m_norm_w, w_out = (
        _np.asarray(a) for a in (x, norm_w, w_in, b_gates, q_norm_w, k_norm_w, m_norm_w, w_out))
    w = w_in[0]
    qa, ka, va, za, qm, km, vm, om, zm, g = _np.split(
        w, _np.cumsum([1024, 1024, 1024, 1024, 512, 512, 1024, 1024, 1024]).tolist(), axis=1)
    gates = _np.zeros((D_MODEL, P), w.dtype)
    bias = _np.zeros(P, w.dtype)
    for at, k in ((0, 0), (64, 1), (32, 2), (96, 3)):
        gates[:, at:at + M_HEADS] = g[:, k * M_HEADS:(k + 1) * M_HEADS]
        bias[at:at + M_HEADS] = b_gates[0, k * M_HEADS:(k + 1) * M_HEADS]
    cols = [gates]
    for j in range(M_HEADS):
        cols += [vm[:, 256 * j:256 * (j + 1)], km[:, P * j:P * (j + 1)], qm[:, P * j:P * (j + 1)],
                 om[:, 256 * j:256 * (j + 1)], zm[:, 256 * j:256 * (j + 1)]]
    for h in range(ATT_HEADS):
        cols += [a[:, P * h:P * (h + 1)] for a in (va, qa, ka)]
    cols.append(za)
    wo = w_out[0].reshape(2, ATT_HEADS, P, D_MODEL).transpose(1, 0, 2, 3).reshape(D_MODEL, D_MODEL)
    w_all = _np.ascontiguousarray(weight_pieces(_np.concatenate(cols + [wo], axis=1)))
    rope, table, eye, tri = shape_constants()
    vecs = _np.zeros((P, 8), w.dtype)
    vecs[:, 0], vecs[:, 1], vecs[:, 2] = q_norm_w[0], k_norm_w[0], bias
    arrays = {
        "xT_dram": _np.ascontiguousarray(x[0].T).reshape(KT, P, SEQ),
        "w_all_dram": w_all,
        "vecs_dram": vecs,
        "norm_cols_dram": _np.ascontiguousarray(norm_w[0].reshape(KT, P).T),
        "m_cols_dram": _np.ascontiguousarray(m_norm_w[0].reshape(8, P).T),
        "att_mask_dram": table,
        "rope_dram": rope,
        "eye_dram": eye,
        "tri_dram": tri,
    }
    nc = _bacc.Bacc("TRN2", target_bir_lowering=False, num_devices=1)
    args = [nc.dram_tensor(n, a.shape, _mybir.dt.float32, kind="ExternalInput").ap() for n, a in arrays.items()]
    y_dram = nc.dram_tensor("y_dram", (KT, P, SEQ), _mybir.dt.float32, kind="Internal").ap()
    outT = nc.dram_tensor("outT_dram", (O_TILES, P, SEQ), _mybir.dt.float32, kind="ExternalOutput").ap()
    build_program(nc, *args, y_dram, outT)
    r = _run(nc, [arrays], core_ids=[0])
    return _np.ascontiguousarray(r.results[0]["outT_dram"].reshape(D_MODEL, SEQ).T).reshape(1, SEQ, D_MODEL)
```
